# Optimizing a Trainium2 kernel written in Bass

```python
import math
import jax, jax.numpy as jnp
from jax import lax
import numpy as np

D_MODEL = 1024
BATCH = 1
SEQ = 256
DEPTH = 2

D_FF = 2816
NORM_EPS = 1e-6

HEAD_DIM = 64
ATT_PATTERNS = ((128, 1), (512, 4), (2048, 16))
N_ATT_GROUPS = len(ATT_PATTERNS)
HEADS_PER_GROUP = 8
N_ATT_HEADS = N_ATT_GROUPS * HEADS_PER_GROUP
ATT_OUT_DIM = HEADS_PER_GROUP * HEAD_DIM
ROPE_THETA = 10000.0

SSM_EXPAND = 2
D_INNER = SSM_EXPAND * D_MODEL
SSM_HEAD_DIM = 64
N_SSM_HEADS = D_INNER // SSM_HEAD_DIM
N_SSM_GROUPS = 4
HEADS_PER_SSM_GROUP = N_SSM_HEADS // N_SSM_GROUPS
D_STATE = 128
CONV_WIDTH = 4
SSD_CHUNK = 128
XBC_DIM = D_INNER + 2 * N_SSM_GROUPS * D_STATE

QKV_COLS = N_ATT_HEADS * HEAD_DIM
IN_SIZES = (QKV_COLS, QKV_COLS, QKV_COLS, D_INNER, XBC_DIM, N_SSM_HEADS, 2 * D_MODEL)
IN_SPLITS = tuple(int(v) for v in np.cumsum(IN_SIZES)[:-1])
N_IN = int(sum(IN_SIZES))

kernel_name = "hybrid_dilated_attn_ssd_macaron"

def rms_norm_f32(x, w):
    xf = x.astype(jnp.float32)
    y = xf * lax.rsqrt(jnp.mean(xf * xf, axis=-1, keepdims=True) + NORM_EPS)
    return y * w.astype(jnp.float32)

def swiglu(h, w_gate, w_up, w_down):
    return (jax.nn.silu(h @ w_gate) * (h @ w_up)) @ w_down

def rope(t, cos, sin):
    half = t.shape[-1] // 2
    t1, t2 = t[..., :half], t[..., half:]
    c = cos[None, :, None, None, :]
    s = sin[None, :, None, None, :]
    return jnp.concatenate([t1 * c - t2 * s, t2 * c + t1 * s], axis=-1)

def dilated_attention(q, k, v, dilation, band):
    bsz, s, h, hd = q.shape
    span = dilation * band
    s_pad = -(-s // span) * span
    sub_len = s_pad // dilation
    nb = sub_len // band

    def to_blocks(t):
        t = jnp.pad(t, ((0, 0), (0, s_pad - s), (0, 0), (0, 0)))
        t = t.reshape(bsz, sub_len, dilation, h, hd)
        t = t.transpose(0, 2, 3, 1, 4)
        return t.reshape(bsz, dilation, h, nb, band, hd)

    def with_prev(t):
        prev = jnp.pad(t, ((0, 0), (0, 0), (0, 0), (1, 0), (0, 0), (0, 0)))[:, :, :, :-1]
        return jnp.concatenate([prev, t], axis=4)

    qb = to_blocks(q)
    kk = with_prev(to_blocks(k))
    vv = with_prev(to_blocks(v))
    scores = jnp.einsum('bdhnqe,bdhnke->bdhnqk', qb, kk) * (hd ** -0.5)
    iq = jnp.arange(band)[:, None]
    ik = jnp.arange(2 * band)[None, :]
    rel = band + iq - ik
    band_ok = (rel >= 0) & (rel <= band)
    key_ok = (jnp.arange(nb)[:, None, None] * band - band + ik[None]) >= 0
    valid = band_ok[None] & key_ok
    scores = jnp.where(valid, scores, -jnp.inf)
    lse = jax.nn.logsumexp(scores, axis=-1)
    p = jnp.exp(scores - lse[..., None])
    o = jnp.einsum('bdhnqk,bdhnke->bdhnqe', p, vv)
    o = o.reshape(bsz, dilation, h, sub_len, hd).transpose(0, 3, 1, 2, 4)
    o = o.reshape(bsz, s_pad, h, hd)[:, :s]
    lse = lse.reshape(bsz, dilation, h, sub_len).transpose(0, 3, 1, 2)
    lse = lse.reshape(bsz, s_pad, h)[:, :s]
    return o, lse

def ssd_chunked_scan(x, dt, a, b_mat, c_mat):
    bsz, s, g, r, p = x.shape
    n = b_mat.shape[-1]
    nc = s // SSD_CHUNK

    def to_chunks(t):
        return jnp.moveaxis(t.reshape(bsz, nc, SSD_CHUNK, *t.shape[2:]), 1, 0)

    idx = jnp.arange(SSD_CHUNK)
    causal = idx[:, None] >= idx[None, :]

    def step(state, inp):
        xc, dtc, bc, cc = inp
        cum = jnp.cumsum(dtc * a, axis=1)
        cum_t = jnp.moveaxis(cum, 1, -1)
        diff = cum_t[..., :, None] - cum_t[..., None, :]
        decay = jnp.exp(jnp.where(causal, diff, -jnp.inf))
        cb = jnp.einsum('bign,bjgn->bgij', cc, bc)
        xdt = xc * dtc[..., None]
        y_diag = jnp.einsum('bgrij,bjgrp->bigrp', cb[:, :, None] * decay, xdt)
        y_off = jnp.einsum('bign,bgrpn->bigrp', cc, state) * jnp.exp(cum)[..., None]
        last = cum[:, -1]
        w_end = jnp.exp(last[:, None] - cum)
        new_state = state * jnp.exp(last)[..., None, None] + jnp.einsum(
            'bjgn,bjgrp->bgrpn', bc, xdt * w_end[..., None])
        return new_state, y_diag + y_off

    state0 = jnp.zeros((bsz, g, r, p, n), jnp.float32)
    xs = (to_chunks(x), to_chunks(dt), to_chunks(b_mat), to_chunks(c_mat))
    _, ys = lax.scan(step, state0, xs)
    return jnp.moveaxis(ys, 0, 1).reshape(bsz, s, g, r, p)

def setup_inputs(seed: int = 0) -> dict:
    key = jax.random.key(seed)
    ks = jax.random.split(key, 24)

    def normal(k, shape, scale):
        return jax.random.normal(k, shape, jnp.float32) * scale

    def gain(k, shape):
        return 1.0 + 0.02 * jax.random.normal(k, shape, jnp.float32)

    dt0 = jnp.exp(jax.random.uniform(ks[13], (DEPTH, N_SSM_HEADS), jnp.float32)
                  * (math.log(0.1) - math.log(0.001)) + math.log(0.001))
    dt0 = jnp.maximum(dt0, 1e-4)
    return {
        'x': normal(ks[0], (BATCH, SEQ, D_MODEL), 1.0),
        'ffn1_norm_w': gain(ks[1], (DEPTH, D_MODEL)),
        'ffn1_w_gate': normal(ks[2], (DEPTH, D_MODEL, D_FF), D_MODEL ** -0.5),
        'ffn1_w_up': normal(ks[3], (DEPTH, D_MODEL, D_FF), D_MODEL ** -0.5),
        'ffn1_w_down': normal(ks[4], (DEPTH, D_FF, D_MODEL), D_FF ** -0.5),
        'mix_norm_w': gain(ks[5], (DEPTH, D_MODEL)),
        'w_in': normal(ks[6], (DEPTH, D_MODEL, N_IN), D_MODEL ** -0.5),
        'b_gates': normal(ks[7], (DEPTH, 2 * D_MODEL), 0.01),
        'q_norm_w': gain(ks[8], (DEPTH, HEAD_DIM)),
        'k_norm_w': gain(ks[9], (DEPTH, HEAD_DIM)),
        'conv_w': normal(ks[10], (DEPTH, CONV_WIDTH, XBC_DIM), CONV_WIDTH ** -0.5),
        'conv_b': normal(ks[11], (DEPTH, XBC_DIM), 0.01),
        'dt_bias': dt0 + jnp.log(-jnp.expm1(-dt0)),
        'a_log': jnp.log(jax.random.uniform(ks[12], (DEPTH, N_SSM_HEADS), jnp.float32, 1.0, 16.0)),
        'd_skip': gain(ks[14], (DEPTH, N_SSM_HEADS)),
        'ssm_norm_w': gain(ks[15], (DEPTH, D_INNER)),
        'w_att_proj': normal(ks[16], (DEPTH, ATT_OUT_DIM, D_MODEL), ATT_OUT_DIM ** -0.5),
        'w_ssm_proj': normal(ks[17], (DEPTH, D_INNER, D_MODEL), D_INNER ** -0.5),
        'w_out': normal(ks[18], (DEPTH, D_MODEL, D_MODEL), D_MODEL ** -0.5),
        'ffn2_norm_w': gain(ks[19], (DEPTH, D_MODEL)),
        'ffn2_w_gate': normal(ks[20], (DEPTH, D_MODEL, D_FF), D_MODEL ** -0.5),
        'ffn2_w_up': normal(ks[21], (DEPTH, D_MODEL, D_FF), D_MODEL ** -0.5),
        'ffn2_w_down': normal(ks[22], (DEPTH, D_FF, D_MODEL), D_FF ** -0.5),
    }

def reference(x, ffn1_norm_w, ffn1_w_gate, ffn1_w_up, ffn1_w_down, mix_norm_w, w_in, b_gates,
              q_norm_w, k_norm_w, conv_w, conv_b, dt_bias, a_log, d_skip, ssm_norm_w,
              w_att_proj, w_ssm_proj, w_out, ffn2_norm_w, ffn2_w_gate, ffn2_w_up, ffn2_w_down):
    bsz, s, _ = x.shape
    dtype = x.dtype
    pos = jnp.arange(s, dtype=jnp.float32)
    inv_freq = 1.0 / (ROPE_THETA ** (jnp.arange(0, HEAD_DIM, 2, dtype=jnp.float32) / HEAD_DIM))
    ang = pos[:, None] * inv_freq[None, :]
    cos, sin = jnp.cos(ang), jnp.sin(ang)

    for i in range(DEPTH):
        h = rms_norm_f32(x, ffn1_norm_w[i]).astype(dtype)
        x = x + (0.5 * swiglu(h, ffn1_w_gate[i], ffn1_w_up[i], ffn1_w_down[i])).astype(dtype)

        h = rms_norm_f32(x, mix_norm_w[i]).astype(dtype)
        proj = h @ w_in[i]
        q, k, v, z, xbc, dt_raw, gate_pre = jnp.split(proj, IN_SPLITS, axis=-1)

        att_shape = (bsz, s, N_ATT_GROUPS, HEADS_PER_GROUP, HEAD_DIM)
        q = rope(rms_norm_f32(q.reshape(att_shape), q_norm_w[i]), cos, sin)
        k = rope(rms_norm_f32(k.reshape(att_shape), k_norm_w[i]), cos, sin)
        v = v.reshape(att_shape).astype(jnp.float32)
        outs, lses = [], []
        for g, (window, dilation) in enumerate(ATT_PATTERNS):
            o_g, lse_g = dilated_attention(q[:, :, g], k[:, :, g], v[:, :, g], dilation, window // dilation)
            outs.append(o_g)
            lses.append(lse_g)
        alpha = jax.nn.softmax(jnp.stack(lses), axis=0)
        att = jnp.sum(alpha[..., None] * jnp.stack(outs), axis=0)
        y_att = att.reshape(bsz, s, ATT_OUT_DIM).astype(dtype) @ w_att_proj[i]

        xbc = lax.conv_general_dilated(
            xbc.astype(jnp.float32), conv_w[i].astype(jnp.float32)[:, None, :],
            window_strides=(1,), padding=[(CONV_WIDTH - 1, 0)],
            dimension_numbers=('NWC', 'WIO', 'NWC'), feature_group_count=XBC_DIM)
        xbc = jax.nn.silu(xbc + conv_b[i].astype(jnp.float32))
        x_ssm, b_mat, c_mat = jnp.split(xbc, (D_INNER, D_INNER + N_SSM_GROUPS * D_STATE), axis=-1)
        x_ssm = x_ssm.reshape(bsz, s, N_SSM_GROUPS, HEADS_PER_SSM_GROUP, SSM_HEAD_DIM)
        b_mat = b_mat.reshape(bsz, s, N_SSM_GROUPS, D_STATE)
        c_mat = c_mat.reshape(bsz, s, N_SSM_GROUPS, D_STATE)
        dt = jax.nn.softplus(dt_raw.astype(jnp.float32) + dt_bias[i].astype(jnp.float32))
        dt = dt.reshape(bsz, s, N_SSM_GROUPS, HEADS_PER_SSM_GROUP)
        a = -jnp.exp(a_log[i].astype(jnp.float32)).reshape(N_SSM_GROUPS, HEADS_PER_SSM_GROUP)
        y = ssd_chunked_scan(x_ssm, dt, a, b_mat, c_mat)
        y = y + d_skip[i].astype(jnp.float32).reshape(N_SSM_GROUPS, HEADS_PER_SSM_GROUP)[..., None] * x_ssm
        y = y.reshape(bsz, s, D_INNER) * jax.nn.silu(z.astype(jnp.float32))
        y = rms_norm_f32(y.reshape(bsz, s, N_SSM_GROUPS, D_INNER // N_SSM_GROUPS),
                         ssm_norm_w[i].reshape(N_SSM_GROUPS, D_INNER // N_SSM_GROUPS))
        y_ssm = y.reshape(bsz, s, D_INNER).astype(dtype) @ w_ssm_proj[i]

        gates = jax.nn.sigmoid(gate_pre.astype(jnp.float32) + b_gates[i].astype(jnp.float32))
        g_att, g_ssm = jnp.split(gates, 2, axis=-1)
        mixed = (g_att * y_att.astype(jnp.float32) + g_ssm * y_ssm.astype(jnp.float32)).astype(dtype)
        x = x + (mixed @ w_out[i]).astype(dtype)

        h = rms_norm_f32(x, ffn2_norm_w[i]).astype(dtype)
        x = x + (0.5 * swiglu(h, ffn2_w_gate[i], ffn2_w_up[i], ffn2_w_down[i])).astype(dtype)
    return x


_drawn_inputs = setup_inputs


def setup_inputs(seed=0):
    import zlib

    import numpy as np

    out = dict(_drawn_inputs(seed))
    spreads = {}
    factors = {'ffn1_norm_w': 3.974,
     'b_gates': 8.0,
     'q_norm_w': 8.0,
     'k_norm_w': 8.0,
     'conv_b': 6.08,
     'd_skip': 6.319,
     'ssm_norm_w': 4.081,
     'ffn2_norm_w': 5.615}
    for name, (base, spread) in spreads.items():
        noise = np.random.default_rng([zlib.crc32(name.encode()), seed]).standard_normal(out[name].shape)
        drawn = base * np.exp(spread * noise) if base else spread * noise
        out[name] = __import__('jax').numpy.asarray(drawn.astype(out[name].dtype))
    for name, factor in factors.items():
        out[name] = (out[name] * factor).astype(out[name].dtype)
    return out
```

```python
from contextlib import ExitStack

import numpy as np
import concourse.bass as bass
from concourse import mybir

F32 = mybir.dt.float32
F32R = mybir.dt.float32r
ALU = mybir.AluOpType
ACT = mybir.ActivationFunctionType
LN_EXP = "natural_log_exp_and_others"

P = 128
SEQ = 256
TILES = SEQ // P
DEPTH = 2
D_MODEL = 1024
KT = D_MODEL // P
D_FF = 2816
EPS = 1e-6
HEAD_DIM = 64
HALF = HEAD_DIM // 2
GROUPS = 3
SLOTS = 8
N_ATT_HEADS = GROUPS * SLOTS
QKV = N_ATT_HEADS * HEAD_DIM
ATT_DIM = SLOTS * HEAD_DIM
D_INNER = 2 * D_MODEL
SSM_HEADS = D_INNER // 64
SSM_GROUPS = 4
STATE = 128
TAPS = 4
XBC = D_INNER + 2 * SSM_GROUPS * STATE
N_IN = 3 * QKV + D_INNER + XBC + SSM_HEADS + 2 * D_MODEL
SCALE = HEAD_DIM ** -0.5
NEG = -1.0e30

PC = 256
PE_LEN = KT * PC
FI = D_FF // PC
Q_AT, K_AT, V_AT = 0, QKV, 2 * QKV
Z_AT = 3 * QKV
XBC_AT = Z_AT + D_INNER
DT_AT = XBC_AT + XBC
GATE_AT = DT_AT + SSM_HEADS
XBC_P = [8, 9, 10, 11] + list(range(8))
COLS = ([XBC_AT + PC * i for i in XBC_P] + [Q_AT + PC * i for i in range(6)] + [K_AT + PC * i for i in range(6)]
        + [V_AT + PC * i for i in range(6)] + [Z_AT + PC * i for i in range(8)] + [GATE_AT + PC * i for i in range(8)])
N_XBC = 0
N_QK = len(XBC_P)
N_V = N_QK + 12
N_Z = N_V + 6
N_G = N_Z + 8
N_ATT = N_G + 8
N_SSM = N_ATT + 2
N_OUT = N_SSM + 8
N_MIX = N_OUT + 4
Y_SPLIT = (N_G + 3, N_G + 4, N_SSM + 2, N_SSM + 4)
SLOT_OF = (0, 2, 1)
GATE_SLOT, DOWN_SLOT, UP_SLOT = 0, 1, 2
USES = 2 * FI + N_MIX // 3

C_CONVW, C_CONVB, C_N1, C_NM, C_N2, C_SSM, C_BG, C_DSK = 0, 96, 120, 128, 136, 144, 160, 176
C_DTB, C_ALOG, C_QK = 192, 224, 256
NPRM = 260
ROWS_A, ROWS_B = 120, 56
NROW = 3 * SSM_HEADS + 2 * HEAD_DIM

K_ID, K_BLK, K_TRI, K_ONE, K_MASK, K_CS, K_SEL, K_NEG = 0, 128, 256, 384, 512, 1280, 1792, 1824
NKEPT = K_SEL
NCONST = 1952


def constants():
    c = np.zeros((P, NCONST), np.float32)
    p = np.arange(P)
    c[:, K_ID:K_ID + P] = np.eye(P)
    c[:, K_ONE:K_ONE + P] = 1.0
    c[:, K_BLK:K_BLK + P] = (p[:, None] // HALF == p[None, :] // HALF)
    c[:, K_TRI:K_TRI + P] = (p[:, None] <= p[None, :])
    for g, (window, dil) in enumerate(((128, 1), (512, 4), (2048, 16))):
        q = np.arange(P, SEQ)[:, None]
        k = np.arange(SEQ)[None, :]
        ok = (k <= q) & (q - k <= window) & ((q - k) % dil == 0)
        c[:, K_MASK + g * SEQ:K_MASK + (g + 1) * SEQ] = np.where(ok, 0.0, NEG)
    inv = (1.0 / (np.float32(10000.0) ** (np.arange(0, HEAD_DIM, 2, dtype=np.float32) / np.float32(HEAD_DIM)))).astype(np.float32)
    ang = (np.arange(SEQ, dtype=np.float32)[None, :] * inv[:, None]).astype(np.float32).astype(np.float64)
    c[:, K_CS:K_CS + SEQ] = np.tile(np.cos(ang), (4, 1))
    c[:, K_CS + SEQ:K_CS + 2 * SEQ] = np.tile(np.sin(ang), (4, 1))
    c[:2 * SSM_HEADS, K_SEL:K_SEL + SSM_HEADS] = np.tile(np.eye(SSM_HEADS), (2, 1))
    c[:, K_NEG:K_NEG + P] = np.where(p[:, None] > p[None, :], NEG, 0.0)
    return c


class Signal:

    def __init__(self, sem, per_layer, before=0, unit=1):
        self.sem, self.per_layer, self.before, self.unit, self.seen = sem, per_layer, before, unit, 0

    def at(self, layer, count):
        return layer * (self.per_layer * self.unit) + (self.before + count) * self.unit

    def one(self, times=1):
        self.seen += times
        return self.sem, self.unit


def halves_in(tile, f):
    return tile[:, :].rearrange("p (kh f c) -> p kh f c", f=2, c=HALF)[:, :, f, :].rearrange("p (k h) c -> p k h c", h=4)


def halves_out(tile, f):
    return tile[:, :].rearrange("p (k f h c) -> p k f h c", f=2, h=4, c=HALF)[:, :, f, :, :]


def program(nc, x, n1w, w1g, w1u, w1d, nmw, w_in, b_gates, q_norm, k_norm, conv_w, conv_b, dt_bias, a_log,
            d_skip, ssm_w, w_att, w_ssm, w_out, n2w, w2g, w2u, w2d, consts, out):
    with ExitStack() as ctx:
        def sb(name, shape, dt=F32):
            return ctx.enter_context(nc.sbuf_tensor(name, shape, dt))

        signals = []

        def signal(name, per_layer, before=0, unit=1):
            s = Signal(ctx.enter_context(nc.semaphore(name)), per_layer, before, unit)
            signals.append(s)
            return s

        con = sb("con", [P, NKEPT])
        con_r = sb("con_r", [P, 288], F32R)
        xT = sb("xT", [P, KT, SEQ])
        hH, hL = sb("hH", [P, KT, SEQ], F32R), sb("hL", [P, KT, SEQ], F32R)
        raw = [sb(f"raw{s}", [P, PE_LEN]) for s in range(3)]
        wH = [sb(f"wH{s}", [P, PE_LEN], F32R) for s in range(3)]
        wL = [sb(f"wL{s}", [P, PE_LEN], F32R) for s in range(3)]
        sq = sb("sq", [P, 4, 512])
        prm_all = sb("prm_all", [P, DEPTH * NPRM])
        prm = sb("prm", [P, NPRM])
        qk = sb("qk", [P, 2, N_ATT_HEADS // 2, SEQ])
        gates = qk[:, :, :, :].rearrange("p a b t -> p (a b) t")
        v = sb("v", [P, TILES, QKV])
        v_flat = v[:, :, :].rearrange("p t n -> p (t n)")
        ht = v_flat[:, 0:KT * SEQ].rearrange("p (k t) -> p k t", k=KT)
        dtw = v_flat[:, 2560:2560 + KT * SSM_HEADS]
        xs = sb("xs", [P, 16, SEQ])
        rows_a = xs[0:ROWS_A, 0:1, :].rearrange("p a (l c) -> p (a l) c", l=DEPTH)
        rows_b = xs[0:ROWS_B, 1:2, :].rearrange("p a (l c) -> p (a l) c", l=DEPTH)
        con_tail = xs[:, 4, 0:NCONST - NKEPT]
        row_r = xs[0:1, 2:4, :].rearrange("p a t -> p (a t)")[:, 0:DEPTH * NROW]
        with (nc.sbuf_tensor("bc", [P, 8, SEQ], F32) as bc,
              nc.sbuf_tensor("qraw", [P, 2, 512], F32) as qraw2, nc.sbuf_tensor("qn", [P, 2, 2, SEQ], F32) as qn2):
            pass
        attH, attL = sb("attH", [P, 4, SEQ], F32R), sb("attL", [P, 4, SEQ], F32R)
        sb("rest", [P, 2048])
        hidH, hidL = (t[:, 0:2, :].rearrange("p a t -> p (a t)") for t in (attH, attL))
        dtwH, dtwL = attH[:, 2, :], attL[:, 2, :]
        with nc.sbuf_tensor("xdt", [P, SSM_GROUPS, TILES, 512], F32) as xdt:
            pass
        yH, yL = sb("yH", [P, 2, 4, SEQ], F32R), sb("yL", [P, 2, 4, SEQ], F32R)
        acc = [sq[:, i, :] for i in range(2)]
        zs = acc
        qraw, qn = [qraw2[:, i, :] for i in range(2)], [qn2[:, i, :, :] for i in range(2)]
        qsq = [sq[:, i, :] for i in range(2)]
        qrs = [sb(f"qrs{i}", [P, SEQ]) for i in range(2)]
        rstd = qrs[0]
        ropa, ropb = (sq[:, i, :].rearrange("p (a t) -> p a t", a=2) for i in (2, 3))
        dtu, dte, dtl, dtm = (qrs[1][:, 64 * i:64 * i + 64] for i in range(4))
        dt, ncum = (sb(n, [P, 64]) for n in ("dt", "ncum"))
        cumr = sb("cumr", [2 * SSM_HEADS, SEQ], F32R)
        cbt = sb("cbt", [P, 384])
        dec = [sb(f"dec{i}", [P, 384]) for i in range(2)]
        scratch = xdt[:, :, :, :].rearrange("p g t n -> p (g t n)")
        sm, pt = scratch[:, 0:1152], scratch[:, 1152:2304]
        att_tok = scratch[:, 2304:3328].rearrange("p (t n) -> p t n", t=TILES)
        dts, dta, aexp = scratch[:, 1152:1216], scratch[:, 1216:1280], scratch[:, 1280:1312]
        sg, hid = scratch[:, 0:512], scratch[:, 512:1024]
        small = sb("small", [P, 16])
        smax, negm, psum_ = (small[:, 2 * i:2 * i + 2] for i in range(3))
        pinv = [small[:, 6 + 2 * i:8 + 2 * i] for i in range(2)]
        eps = small[:, 10:11]
        yrs = qrs
        psm = ctx.enter_context(nc.psum_tensor("psm", [P, 8 * 512], F32))

        att_turned_out = psm[:, 1024:2048].rearrange("p (c t) -> p c t", t=SEQ)

        def bank(b, lo=0, hi=512, p0=0, p1=P):
            return psm[p0:p1, b * 512 + lo:b * 512 + hi]

        ident = con[:, K_ID:K_ID + P]
        ones = con[:, K_ONE:K_ONE + P]
        tri = con[:, K_TRI:K_TRI + SEQ]
        ident_r, neg_r, sel_r = con_r[:, 0:P], con_r[:, P:2 * P], con_r[:, 2 * P:2 * P + 32]

        raw_full = [signal(f"raw_full{s}", USES, unit=16) for s in range(3)]
        hi_ready = [signal(f"hi_ready{s}", USES) for s in range(3)]
        lo_ready = [signal(f"lo_ready{s}", USES, 1) for s in range(3)]
        used = [signal(f"panel_used{s}", USES, 1) for s in range(3)]
        x_ready = signal("x_ready", 12, 0)
        sq_ready, ss_done = signal("sq_ready", 12), signal("ss_done", 3)
        ln_done, rstd_ready = signal("ln_done", 3), signal("rstd_ready", 3)
        hn_ready, hhi, hlo = signal("hn_ready", 12), signal("hhi", 12), signal("hlo", 12)
        acc_done = signal("acc_done", 6)
        silu_done, hid_ready = signal("silu_done", 2 * FI), signal("hid_ready", 2 * FI)
        hidhi, hidlo = signal("hidhi", 2 * FI), signal("hidlo", 2 * FI)
        prm_ready = signal("prm_ready", 1)
        dtw_full, dtw_hi, dtw_lo = signal("dtw_full", 1, 0, 16), signal("dtw_hi", 1), signal("dtw_lo", 1, 1)
        dt_done, cum_done = signal("dt_done", 1), signal("cum_done", 1)
        dt_dve, dt_act = signal("dt_dve", 6), signal("dt_act", 5)
        conv_bias, conv_tap, conv_silu = signal("conv_bias", 24), signal("conv_tap", 72), signal("conv_silu", 12)
        proj_read = signal("proj_read", N_ATT - N_QK)
        qk_ss, qk_ln, qk_rstd = signal("qk_ss", 12), signal("qk_ln", 12), signal("qk_rstd", 12)
        qn_ready, rope_ab, rope_ready = signal("qn_ready", 12), signal("rope_ab", 12), signal("rope_ready", 12)
        xt_done, xdt_ready = signal("xt_done", 8), signal("xdt_ready", 8)
        cb_done, cb_copied = signal("cb_done", 4), signal("cb_copied", 4)
        decay_sum, dec_ready, l_ready = signal("decay_sum", 32), signal("dec_ready", 32), signal("l_ready", 32)
        y_done, ys_ready = signal("y_done", 16), signal("ys_ready", 16)
        s_done, smax_ready, negm_ready = signal("s_done", 8), signal("smax_ready", 16), signal("negm_ready", 8)
        p_exp, p_inv = signal("p_exp", 8), signal("p_inv", 8)
        pt_done, pt_act, pt_dve = signal("pt_done", 8), signal("pt_act", 8), signal("pt_dve", 8)
        pt_last = signal("pt_last", 8)
        pv_done, att_tok_ready, att_turned = signal("pv_done", 8), signal("att_tok_ready", 8), signal("att_turned", 1)
        att_hi, att_lo = signal("att_hi", 1), signal("att_lo", 1)
        qsq_added, ysq_added = signal("qsq_added", 12), signal("ysq_added", 8)
        yz_ready, ysq_ready, yss_done = signal("yz_ready", 8), signal("ysq_ready", 4), signal("yss_done", 4)
        ysln, yrstd, yn_ready = signal("ysln", 4), signal("yrstd", 4), signal("yn_ready", 4)
        yhi, ylo = signal("yhi", 4), signal("ylo", 4)
        att_read, ssm_done, ssm_read = signal("att_read", 4), signal("ssm_done", 3), signal("ssm_read", 4)
        mix_ready, mix_hi, mix_lo = signal("mix_ready", 4), signal("mix_hi", 4), signal("mix_lo", 4)
        ld_con, ld_x, ld_prm = (ctx.enter_context(nc.semaphore(n)) for n in ("ld_con", "ld_x", "ld_prm"))
        con_ready, pro_pe, pro_dve = (ctx.enter_context(nc.semaphore(n)) for n in ("con_ready", "pro_pe", "pro_dve"))
        fin_pe, fin_dve, stored = (ctx.enter_context(nc.semaphore(n)) for n in ("fin_pe", "fin_dve", "stored"))

        sp_turn = ctx.enter_context(nc.semaphore("sp_turn"))

        def use_of(n):
            return FI + n // 3

        block = ctx.enter_context(nc.Block())

        @block.sync
        def _(sp):
            sp.dma_start(con[:, :], consts[:, 0:NKEPT]).then_inc(ld_con, 16)
            sp.dma_start(con_tail, consts[:, NKEPT:NCONST]).then_inc(ld_con, 16)
            xtok = v_flat[:, 0:KT * SEQ]
            sp.dma_start(xtok.rearrange("p (t n) -> p t n", t=TILES),
                         x.rearrange("b (t p) n -> p (b t) n", p=P)).then_inc(ld_x, 16)
            for src, tile, r0, r1 in (
                    (conv_w.rearrange("l k (c p) -> (k c) l p", p=P), rows_a, 0, 96),
                    (conv_b.rearrange("l (c p) -> c l p", p=P), rows_a, 96, 120),
                    (n1w.rearrange("l (c p) -> c l p", p=P), rows_b, 0, 8),
                    (nmw.rearrange("l (c p) -> c l p", p=P), rows_b, 8, 16),
                    (n2w.rearrange("l (c p) -> c l p", p=P), rows_b, 16, 24),
                    (ssm_w.rearrange("l (c p) -> c l p", p=P), rows_b, 24, 40),
                    (b_gates.rearrange("l (c p) -> c l p", p=P), rows_b, 40, 56)):
                if src is None:
                    continue
                sp.dma_start(tile[r0:r1, :, :], src).then_inc(ld_prm, 16)
            rr = row_r[:, :].rearrange("a (l n) -> a l n", l=DEPTH)
            for src, lo, hi in ((d_skip, 0, 32), (dt_bias, 32, 64), (a_log, 64, 96), (q_norm, 96, 160), (k_norm, 160, 224)):
                sp.dma_start(rr[:, :, lo:hi], src.rearrange("(a l) n -> a l n", a=1)).then_inc(ld_prm, 16)

            flat = {id(w): w.rearrange("l r n -> (l r) n") for w in (w1g, w1u, w1d, w2g, w2u, w2d, w_in, w_att, w_ssm, w_out)}

            def load(l, slot, use, w, rows, row0, nrows, col0, ncols):
                sp.wait_ge(lo_ready[slot].sem, lo_ready[slot].at(l, use))
                sp.sem_inc(sp_turn, 1)
                src = flat[id(w)][bass.ds(l * rows + row0, nrows), bass.ds(col0, ncols)]
                sp.dma_start(raw[slot][:, :].rearrange("p (k n) -> p k n", n=ncols),
                             src.rearrange("(k p) n -> p k n", p=P)).then_inc(raw_full[slot].sem, 16)

            def ffn(l, use0, wg, wu, wd):
                def gate(i):
                    load(l, GATE_SLOT, use0 + i, wg, D_MODEL, 0, D_MODEL, i * PC, PC)

                def up(i):
                    load(l, UP_SLOT, use0 + i, wu, D_MODEL, 0, D_MODEL, i * PC, PC)

                def down(i):
                    load(l, DOWN_SLOT, use0 + i, wd, D_FF, i * PC, PC, 0, D_MODEL)

                gate(0)
                up(0)
                with sp.Fori(1, FI) as i:
                    gate(i)
                    down(i - 1)
                    up(i)
                down(FI - 1)

            with sp.Fori(0, DEPTH) as l:
                sp.wait_ge(dtw_lo.sem, dtw_lo.at(l, 0))
                sp.sem_inc(sp_turn, 1)
                sp.dma_start(dtw[:, :].rearrange("p (k n) -> p k n", n=SSM_HEADS),
                             flat[id(w_in)][bass.ds(l * D_MODEL, D_MODEL), DT_AT:DT_AT + SSM_HEADS]
                             .rearrange("(k p) n -> p k n", p=P)).then_inc(dtw_full.sem, 16)
                ffn(l, 0, w1g, w1u, w1d)
                for n in range(N_MIX):
                    slot, use = SLOT_OF[n % 3], use_of(n)
                    if n < N_ATT:
                        load(l, slot, use, w_in, D_MODEL, 0, D_MODEL, COLS[n], PC)
                    elif n < N_SSM:
                        load(l, slot, use, w_att, ATT_DIM, 0, ATT_DIM, (n - N_ATT) * 512, 512)
                    elif n < N_OUT:
                        load(l, slot, use, w_ssm, D_INNER, (n - N_SSM) * PC, PC, 0, D_MODEL)
                    else:
                        load(l, slot, use, w_out, D_MODEL, 0, D_MODEL, (n - N_OUT) * PC, PC)
                ffn(l, USES - FI, w2g, w2u, w2d)

            sp.wait_ge(fin_dve, 2)
            sp.dma_start(out.rearrange("b (t p) n -> p (b t) n", p=P),
                         v_flat[:, 0:KT * SEQ].rearrange("p (t n) -> p t n", t=TILES)).then_inc(stored, 16)
            sp.wait_ge(stored, 16)

        @block.gpsimd
        def _(pool):
            pool.sem_inc(lo_ready[UP_SLOT].sem, 1)

            def split_lo(l, use, times=1):
                s = UP_SLOT
                pool.wait_ge(hi_ready[s].sem, hi_ready[s].at(l, use + 1))
                nc.gpsimd.tensor_tensor(wL[s][:, :], raw[s][:, :], wH[s][:, :], ALU.subtract).then_inc(*lo_ready[s].one(times))

            def split_lo_qk(l, use):
                s = UP_SLOT
                pool.wait_ge(hi_ready[s].sem, hi_ready[s].at(l, use + 1))
                for f in range(2):
                    ins = nc.gpsimd.tensor_tensor(halves_out(wL[s], f), halves_in(raw[s], f), halves_out(wH[s], f), ALU.subtract)
                ins.then_inc(*lo_ready[s].one())

            def rope_products(l, i):
                cs = con[:, K_CS:K_CS + 512].rearrange("p (a t) -> p a t", a=2)
                pool.wait_ge(qn_ready.sem, qn_ready.at(l, i + 1))
                if i >= 1:
                    pool.wait_ge(rope_ready.sem, rope_ready.at(l, i))
                nc.gpsimd.tensor_tensor(ropa[:, :, :], qn[i % 2][:, 0:1, :].to_broadcast([P, 2, SEQ]), cs, ALU.mult)
                nc.gpsimd.tensor_tensor(ropb[:, :, :], qn[i % 2][:, 1:2, :].to_broadcast([P, 2, SEQ]), cs, ALU.mult).then_inc(*rope_ab.one())

            def add_squares(l, i):
                pool.wait_ge(proj_read.sem, proj_read.at(l, i + 1))
                q = qsq[i % 2]
                nc.gpsimd.tensor_tensor(q[:, 0:SEQ], q[:, 0:SEQ], q[:, SEQ:512], ALU.add).then_inc(*qsq_added.one())

            def add_y_squares(l, g):
                a, b = sq[:, 2 * (g % 2), :], sq[:, 2 * (g % 2) + 1, :]
                pool.wait_ge(ysq_ready.sem, ysq_ready.at(l, g + 1))
                nc.gpsimd.tensor_tensor(a, a, b, ALU.add).then_inc(*ysq_added.one())
                pool.wait_ge(ysq_added.sem, ysq_added.at(l, 2 * g + 1))
                nc.gpsimd.tensor_tensor(a[:, 0:SEQ], a[:, 0:SEQ], a[:, SEQ:512], ALU.add).then_inc(*ysq_added.one())

            with pool.Fori(0, DEPTH) as l:
                with pool.Fori(0, FI) as i:
                    split_lo(l, i, FI)
                for s in range(-2, N_MIX - 2):
                    if 0 <= s - 1 - N_QK < 12:
                        add_squares(l, s - 1 - N_QK)
                    if 0 <= s - N_G < SSM_GROUPS:
                        add_y_squares(l, s - N_G)
                    n = s + 2
                    if SLOT_OF[n % 3] == UP_SLOT:
                        (split_lo_qk if N_QK <= n < N_V else split_lo)(l, use_of(n))
                    if 0 <= s - 2 - N_QK < 12:
                        rope_products(l, s - 2 - N_QK)
                with pool.Fori(0, FI) as i:
                    split_lo(l, USES - FI + i, FI)

        @block.scalar
        def _(act):
            act.wait_ge(ld_con, 32)
            act.activation(con_r[:, 0:P], ident, ACT.Copy)
            act.activation(con_r[:, P:2 * P], con_tail[:, K_NEG - NKEPT:K_NEG - NKEPT + P], ACT.Copy)
            act.activation(con_r[:, 2 * P:2 * P + 32], con_tail[:, K_SEL - NKEPT:K_SEL - NKEPT + 32], ACT.Copy).then_inc(con_ready, 1)

            def split_hi(l, s, use, times=1):
                act.wait_ge(raw_full[s].sem, raw_full[s].at(l, use + 1))
                act.wait_ge(used[s].sem, used[s].at(l, use))
                act.activation(wH[s][:, :], raw[s][:, :], ACT.Copy).then_inc(*hi_ready[s].one(times))

            def split_mix(l, n):
                s, use = SLOT_OF[n % 3], use_of(n)
                if not N_QK <= n < N_V:
                    return split_hi(l, s, use)
                act.wait_ge(raw_full[s].sem, raw_full[s].at(l, use + 1))
                act.wait_ge(used[s].sem, used[s].at(l, use))
                for f in range(2):
                    ins = act.activation(halves_out(wH[s], f), halves_in(raw[s], f), ACT.Copy)
                ins.then_inc(*hi_ready[s].one())

            def norm(l, k):
                for j in range(4):
                    act.wait_ge(x_ready.sem, x_ready.at(l, 4 * k + j + 1))
                    act.activation(sq[:, j, :].rearrange("p (c t) -> p c t", c=2), xT[:, 2 * j:2 * j + 2, :], ACT.Square).then_inc(*sq_ready.one())
                act.preload_act_table_set(LN_EXP)
                act.wait_ge(ss_done.sem, ss_done.at(l, k + 1))
                act.activation(rstd[:, :], bank(6, 0, SEQ), ACT.Ln, bias=eps[:, :], scale=1.0 / D_MODEL).then_inc(*ln_done.one())
                act.wait_ge(ln_done.sem, ln_done.at(l, k + 1))
                act.activation(rstd[:, :], rstd[:, :], ACT.Exp, scale=-0.5).then_inc(*rstd_ready.one())
                for j in range(4):
                    act.wait_ge(hn_ready.sem, hn_ready.at(l, 4 * k + j + 1))
                    act.activation(hH[:, 2 * j:2 * j + 2, :], ht[:, 2 * j:2 * j + 2, :], ACT.Copy).then_inc(*hhi.one())

            def ffn(l, f):
                use0, e0 = (0, USES - FI)[f], f * FI

                def hid_hi(i, times=1):
                    act.wait_ge(hid_ready.sem, hid_ready.at(l, e0 + i + 1))
                    act.activation(hidH[:, :], hid[:, :], ACT.Copy).then_inc(*hidhi.one(times))

                def silu(i, times=1):
                    act.wait_ge(used[GATE_SLOT].sem, used[GATE_SLOT].at(l, use0 + i + 1))
                    act.activation(sg[:, :], bank(4), ACT.Silu).then_inc(*silu_done.one(times))

                split_hi(l, GATE_SLOT, use0)
                split_hi(l, UP_SLOT, use0)
                norm(l, 2 * f)
                silu(0)
                split_hi(l, GATE_SLOT, use0 + 1)
                split_hi(l, DOWN_SLOT, use0)
                with act.Fori(1, FI - 1) as i:
                    hid_hi(i - 1, FI - 2)
                    split_hi(l, UP_SLOT, use0 + i, FI - 2)
                    silu(i, FI - 2)
                    split_hi(l, GATE_SLOT, use0 + i + 1, FI - 2)
                    split_hi(l, DOWN_SLOT, use0 + i, FI - 2)
                hid_hi(FI - 2)
                split_hi(l, UP_SLOT, use0 + FI - 1)
                silu(FI - 1)
                split_hi(l, DOWN_SLOT, use0 + FI - 1)
                hid_hi(FI - 1)

            def panel_done(l, n):
                s = SLOT_OF[n % 3]
                act.wait_ge(used[s].sem, used[s].at(l, use_of(n) + 1))

            def dt_steps(l):
                act.wait_ge(dt_dve.sem, dt_dve.at(l, 1))
                act.activation(dtu[:, :], dts[:, :], ACT.Abs).then_inc(*dt_act.one())
                act.wait_ge(dt_act.sem, dt_act.at(l, 1))
                act.activation(dte[:, :], dtu[:, :], ACT.Exp, scale=-1.0).then_inc(*dt_act.one())
                act.wait_ge(dt_act.sem, dt_act.at(l, 2))
                act.activation(dtl[:, :], dte[:, :], ACT.Ln, bias=ones[:, 0:1]).then_inc(*dt_act.one())
                act.activation(aexp[:, :], prm[:, C_ALOG:C_ALOG + 32], ACT.Exp).then_inc(*dt_act.one())

            def evacuate(l, n):
                b = 4 + n % 2
                panel_done(l, n)
                if n < N_QK:
                    ch = 2 * XBC_P[n]
                    if n >= 2:
                        act.wait_ge(conv_silu.sem, conv_silu.at(l, n - 1))
                    for j in range(2):
                        act.activation(acc[n % 2][:, j * SEQ:(j + 1) * SEQ], bank(b, j * SEQ, (j + 1) * SEQ), ACT.Identity,
                                       bias=prm[:, C_CONVB + ch + j:C_CONVB + ch + j + 1],
                                       scale=prm[:, C_CONVW + 72 + ch + j:C_CONVW + 73 + ch + j]).then_inc(*conv_bias.one())
                elif n < N_V:
                    i = n - N_QK
                    if i >= 2:
                        act.wait_ge(qn_ready.sem, qn_ready.at(l, i - 1))
                        act.wait_ge(qk_ss.sem, qk_ss.at(l, i - 1))
                    else:
                        act.wait_ge(conv_silu.sem, conv_silu.at(l, N_QK - 1 + i))
                    act.activation(qraw[i % 2][:, :], bank(b), ACT.Copy)
                    act.activation(qsq[i % 2], bank(b), ACT.Square).then_inc(*proj_read.one())
                elif n < N_Z:
                    c0 = (n - N_V) * PC
                    act.activation(v[:, :, c0:c0 + PC], bank(b).rearrange("p (t c) -> p t c", t=TILES), ACT.Copy).then_inc(*proj_read.one())
                elif n < N_G:
                    i = n - N_Z
                    if i >= 2:
                        act.wait_ge(yz_ready.sem, yz_ready.at(l, i - 1))
                    else:
                        act.wait_ge(qk_ss.sem, qk_ss.at(l, 12))
                    act.activation(zs[i % 2][:, :], bank(b), ACT.Silu).then_inc(*proj_read.one())
                elif n < N_ATT:
                    i = n - N_G
                    act.wait_ge(s_done.sem, s_done.at(l, SLOTS))
                    for j in range(2):
                        ins = act.activation(gates[:, 2 * i + j, :], bank(b, j * SEQ, (j + 1) * SEQ), ACT.Sigmoid,
                                             bias=prm[:, C_BG + 2 * i + j:C_BG + 2 * i + j + 1])
                    ins.then_inc(*proj_read.one())

            def conv_out(l, n):
                c0 = 2 * XBC_P[n]
                dst = xs[:, c0:c0 + 2, :] if c0 < 16 else bc[:, c0 - 16:c0 - 14, :]
                act.wait_ge(conv_tap.sem, conv_tap.at(l, 6 * n + 6))
                act.activation(dst, acc[n % 2][:, :].rearrange("p (c t) -> p c t", c=2), ACT.Silu).then_inc(*conv_silu.one())

            def qk_rms(l, i):
                act.wait_ge(qk_ss.sem, qk_ss.at(l, i + 1))
                if i >= 2:
                    act.wait_ge(qn_ready.sem, qn_ready.at(l, i - 1))
                act.activation(qrs[i % 2][:, :], bank(6, (i % 2) * SEQ, (i % 2 + 1) * SEQ), ACT.Ln, bias=eps[:, :],
                               scale=1.0 / HEAD_DIM).then_inc(*qk_ln.one())
                act.wait_ge(qk_ln.sem, qk_ln.at(l, i + 1))
                act.activation(qrs[i % 2][:, :], qrs[i % 2][:, :], ACT.Exp, scale=-0.5).then_inc(*qk_rstd.one())

            def copy_cb(l, g):
                act.wait_ge(cb_done.sem, cb_done.at(l, g + 1))
                if g >= 1:
                    act.wait_ge(l_ready.sem, l_ready.at(l, 8 * g))
                act.activation(cbt[:, :], bank(7, 0, 384), ACT.Copy).then_inc(*cb_copied.one())

            def decays(l, k):
                for hh in range(2):
                    head = 2 * k + hh
                    act.wait_ge(decay_sum.sem, decay_sum.at(l, head + 1))
                    if k >= 1 and hh == 0:
                        act.wait_ge(y_done.sem, y_done.at(l, k))
                    act.activation(dec[hh][:, 0:256], bank(hh, 0, 256), ACT.Exp, bias=ncum[:, head:head + 1])
                    act.activation(dec[hh][:, 256:384], bank(hh, 256, 384), ACT.Exp,
                                   bias=ncum[:, 32 + head:33 + head]).then_inc(*dec_ready.one())

            def copy_pt(l, sl):
                act.wait_ge(pt_done.sem, pt_done.at(l, sl + 1))
                if sl >= 1:
                    act.wait_ge(pv_done.sem, pv_done.at(l, sl))
                act.activation(pt[:, 0:512], bank(3), ACT.Copy).then_inc(*pt_act.one())

            def attn_hi(l):
                act.wait_ge(att_turned.sem, att_turned.at(l, 1))
                act.activation(attH[:, :, :], att_turned_out, ACT.Copy).then_inc(*att_hi.one())

            def softmax_exp(l, sl):
                act.wait_ge(negm_ready.sem, negm_ready.at(l, sl + 1))
                if sl >= 1:
                    act.wait_ge(p_inv.sem, p_inv.at(l, sl))
                act.activation(sm[:, 0:384], sm[:, 0:384], ACT.Exp, bias=negm[:, 0:1], scale=SCALE, accum_out=psum_[:, 0:1])
                act.activation(sm[:, 384:1152], sm[:, 384:1152], ACT.Exp, bias=negm[:, 1:2], scale=SCALE,
                               accum_out=psum_[:, 1:2]).then_inc(*p_exp.one())

            def y_square(l, g):
                act.wait_ge(yz_ready.sem, yz_ready.at(l, 8))
                if g >= 2:
                    act.wait_ge(yss_done.sem, yss_done.at(l, g - 1))
                act.activation(sq[:, 2 * (g % 2):2 * (g % 2) + 2, :].rearrange("p a (c t) -> p (a c) t", c=2),
                               xs[:, 4 * g:4 * g + 4, :], ACT.Square).then_inc(*ysq_ready.one())

            def y_rms(l, g):
                act.preload_act_table_set(LN_EXP)
                act.wait_ge(yss_done.sem, yss_done.at(l, g + 1))
                if g >= 2:
                    act.wait_ge(yn_ready.sem, yn_ready.at(l, g - 1))
                act.activation(yrs[g % 2][:, :], bank(g % 2, 0, SEQ), ACT.Ln, bias=eps[:, :], scale=1.0 / 512).then_inc(*ysln.one())
                act.wait_ge(ysln.sem, ysln.at(l, g + 1))
                act.activation(yrs[g % 2][:, :], yrs[g % 2][:, :], ACT.Exp, scale=-0.5).then_inc(*yrstd.one())

            def y_hi(l, g):
                act.wait_ge(yn_ready.sem, yn_ready.at(l, g + 1))
                if g >= 2:
                    n = N_SSM + 2 * (g - 2) + 1
                    panel_done(l, n)
                act.activation(yH[:, g % 2, :, :], xs[:, 4 * g:4 * g + 4, :], ACT.Copy).then_inc(*yhi.one())

            def mixer(l):
                split_mix(l, 0)
                split_mix(l, 1)
                act.wait_ge(dtw_full.sem, dtw_full.at(l, 1))
                act.activation(dtwH[:, :], dtw[:, :], ACT.Copy).then_inc(*dtw_hi.one())
                norm(l, 1)
                dt_steps(l)
                for s in range(N_OUT):
                    if 0 <= s - 1 < N_ATT:
                        evacuate(l, s - 1)
                    if 0 <= s - 2 < N_QK:
                        conv_out(l, s - 2)
                    if s == 3:
                        act.wait_ge(cum_done.sem, cum_done.at(l, 1))
                        act.activation(cumr[0:32, :], bank(7, 64, 320, 0, 32), ACT.Copy).then_inc(*dt_act.one())
                    t = s - N_QK
                    if t == 2:
                        act.preload_act_table_set(LN_EXP)
                    if 0 <= t - 2 < 12:
                        qk_rms(l, t - 2)
                    if 0 <= t - 1 < 16:
                        decays(l, t - 1)
                    if t >= 0 and t % 4 == 0 and t // 4 < SSM_GROUPS:
                        copy_cb(l, t // 4)
                    u = s - N_Z
                    if 0 <= u - 1 < SLOTS:
                        copy_pt(l, u - 1)
                    if u == SLOTS + 3:
                        attn_hi(l)
                    if 0 <= u < SLOTS:
                        softmax_exp(l, u)
                    w = s - N_G
                    if 0 <= w - 1 < 4:
                        y_square(l, w - 1)
                    if 0 <= w - 2 < 4:
                        y_rms(l, w - 2)
                    if s in Y_SPLIT:
                        y_hi(l, Y_SPLIT.index(s))
                    if s + 2 <= N_OUT:
                        split_mix(l, s + 2)
                for j in range(4):
                    mixed_hi(l, j)
                for n in range(N_OUT + 1, N_MIX):
                    split_mix(l, n)

            def mixed_hi(l, j):
                act.wait_ge(mix_ready.sem, mix_ready.at(l, j + 1))
                act.activation(hH[:, 2 * j:2 * j + 2, :], gates[:, 2 * j:2 * j + 2, :], ACT.Copy).then_inc(*mix_hi.one())

            act.wait_ge(pro_dve, 1)
            with act.Fori(0, DEPTH) as l:
                act.wait_ge(prm_ready.sem, prm_ready.at(l, 1))
                ffn(l, 0)
                mixer(l)
                ffn(l, 1)

        @block.vector
        def _(dve):
            dve.sem_inc(lo_ready[0].sem, 1)
            dve.sem_inc(lo_ready[1].sem, 1)
            dve.sem_inc(dtw_lo.sem, 1)
            dve.memset(eps[:, :], EPS)
            dve.wait_ge(pro_pe, 1)
            for l in range(DEPTH):
                c = l * NPRM
                dve.tensor_copy(prm_all[:, c:c + 120], bank(4, l * 120, l * 120 + 120))
                dve.tensor_copy(prm_all[:, c + 120:c + 176], bank(4, 240 + l * 56, 296 + l * 56))
                for r in range(2):
                    dve.tensor_copy(prm_all[64 * r:64 * r + 64, c + C_DSK:c + C_DSK + 16],
                                    bank(5, l * 96, l * 96 + 32, 64 * r, 64 * r + 64).rearrange("p (c r) -> p c r", r=2)[:, :, r])
                dve.tensor_copy(prm_all[:, c + C_DTB:c + C_DTB + 64], bank(5, l * 96 + 32, l * 96 + 96))
                ins = dve.tensor_copy(prm_all[:, c + C_QK:c + C_QK + 4], bank(5, 192 + 4 * l, 196 + 4 * l))
            ins.then_inc(pro_dve, 1)
            for j in range(4):
                dve.wait_ge(pro_pe, 2 + j)
                dve.tensor_copy(xT[:, 2 * j:2 * j + 2, :], bank(j).rearrange("p (c t) -> p c t", c=2)).then_inc(x_ready.sem, 1)
            dve.wait_ge(pro_dve, 1)

            def split_lo(l, s, use, times=1):
                dve.wait_ge(hi_ready[s].sem, hi_ready[s].at(l, use + 1))
                dve.tensor_tensor(wL[s][:, :], raw[s][:, :], wH[s][:, :], ALU.subtract).then_inc(*lo_ready[s].one(times))

            def split_mix(l, n):
                s = SLOT_OF[n % 3]
                if s == UP_SLOT:
                    return
                if not N_QK <= n < N_V:
                    return split_lo(l, s, use_of(n))
                dve.wait_ge(hi_ready[s].sem, hi_ready[s].at(l, use_of(n) + 1))
                for f in range(2):
                    ins = dve.tensor_tensor(halves_out(wL[s], f), halves_in(raw[s], f), halves_out(wH[s], f), ALU.subtract)
                ins.then_inc(*lo_ready[s].one())

            def residual(l, r, scale):
                for j in range(4):
                    if r == 1:
                        n = N_OUT + j
                        dve.wait_ge(used[SLOT_OF[n % 3]].sem, used[SLOT_OF[n % 3]].at(l, use_of(n) + 1))
                    elif j < 3:
                        dve.wait_ge(acc_done.sem, acc_done.at(l, 3 * (r // 2) + j + 1))
                    else:
                        dve.wait_ge(used[DOWN_SLOT].sem, used[DOWN_SLOT].at(l, USES if r else FI))
                    xj = xT[:, 2 * j:2 * j + 2, :]
                    dve.scalar_tensor_tensor(out=xj, in0=bank(j).rearrange("p (c t) -> p c t", c=2), scalar=scale, in1=xj,
                                             op0=ALU.mult, op1=ALU.add).then_inc(*x_ready.one())

            def norm(l, k, col):
                def lo(j):
                    dve.wait_ge(hhi.sem, hhi.at(l, 4 * k + j + 1))
                    dve.tensor_tensor(hL[:, 2 * j:2 * j + 2, :], ht[:, 2 * j:2 * j + 2, :], hH[:, 2 * j:2 * j + 2, :],
                                      ALU.subtract).then_inc(*hlo.one())

                dve.wait_ge(x_ready.sem, x_ready.at(l, 4 * k + 4))
                dve.wait_ge(rstd_ready.sem, rstd_ready.at(l, k + 1))
                for j in range(4):
                    for c in (2 * j, 2 * j + 1):
                        ins = dve.scalar_tensor_tensor(out=ht[:, c, :], in0=xT[:, c, :], scalar=prm[:, col + c:col + c + 1],
                                                       in1=rstd[:, :], op0=ALU.mult, op1=ALU.mult)
                    ins.then_inc(*hn_ready.one())
                    if j >= 1:
                        lo(j - 1)
                lo(3)

            def ffn(l, f):
                use0, e0 = (0, USES - FI)[f], f * FI

                def hidden(i, times=1):
                    dve.wait_ge(silu_done.sem, silu_done.at(l, e0 + i + 1))
                    dve.wait_ge(used[UP_SLOT].sem, used[UP_SLOT].at(l, use0 + i + 1))
                    dve.tensor_tensor(hid[:, :], bank(5), sg[:, :], ALU.mult).then_inc(*hid_ready.one(times))
                    dve.wait_ge(hidhi.sem, hidhi.at(l, e0 + i + 1))
                    dve.tensor_tensor(hidL[:, :], hid[:, :], hidH[:, :], ALU.subtract).then_inc(*hidlo.one(times))

                split_lo(l, GATE_SLOT, use0)
                if f:
                    residual(l, 1, 1.0)
                norm(l, 2 * f, C_N2 if f else C_N1)
                split_lo(l, GATE_SLOT, use0 + 1)
                split_lo(l, DOWN_SLOT, use0)
                with dve.Fori(1, FI - 1) as i:
                    hidden(i - 1, FI - 2)
                    split_lo(l, GATE_SLOT, use0 + i + 1, FI - 2)
                    split_lo(l, DOWN_SLOT, use0 + i, FI - 2)
                hidden(FI - 2)
                split_lo(l, DOWN_SLOT, use0 + FI - 1)
                hidden(FI - 1)

            def taps(l, n):
                b, ch = 4 + n % 2, 2 * XBC_P[n]
                for d in range(1, TAPS):
                    for j in range(2):
                        k = 2 * (d - 1) + j
                        if d == 1:
                            dve.wait_ge(conv_bias.sem, conv_bias.at(l, 2 * n + 2))
                        else:
                            dve.wait_ge(conv_tap.sem, conv_tap.at(l, 6 * n + k - 1))
                        a = acc[n % 2][:, j * SEQ + d:(j + 1) * SEQ]
                        col = C_CONVW + (TAPS - 1 - d) * 24 + ch + j
                        dve.scalar_tensor_tensor(out=a, in0=bank(b, j * SEQ, (j + 1) * SEQ - d), scalar=prm[:, col:col + 1], in1=a,
                                                 op0=ALU.mult, op1=ALU.add).then_inc(*conv_tap.one())

            def qk_norm(l, i):
                w = C_QK + 2 * (i // 6)
                dve.wait_ge(qk_rstd.sem, qk_rstd.at(l, i + 1))
                if i >= 2:
                    dve.wait_ge(rope_ab.sem, rope_ab.at(l, i - 1))
                for f in range(2):
                    ins = dve.scalar_tensor_tensor(out=qn[i % 2][:, f, :], in0=qraw[i % 2][:, f * SEQ:(f + 1) * SEQ],
                                                   scalar=prm[:, w + f:w + f + 1], in1=qrs[i % 2][:, :], op0=ALU.mult, op1=ALU.mult)
                ins.then_inc(*qn_ready.one())

            def rope(l, i):
                which, c = i // 6, i % 6
                dve.wait_ge(rope_ab.sem, rope_ab.at(l, i + 1))
                for h in range(4):
                    r, to = slice(32 * h, 32 * h + 32), 64 * (h % 2)
                    chunk = 2 * c + h // 2
                    dve.tensor_tensor(qk[to:to + 32, which, chunk, :], ropa[r, 0, :], ropb[r, 1, :], ALU.subtract)
                    ins = dve.tensor_tensor(qk[to + 32:to + 64, which, chunk, :], ropb[r, 0, :], ropa[r, 1, :], ALU.add)
                ins.then_inc(*rope_ready.one())

            def x_times_dt(l, g, tile):
                dve.wait_ge(xt_done.sem, xt_done.at(l, 2 * g + tile + 1))
                d = dt[:, 32 * tile + 8 * g:32 * tile + 8 * g + 8].rearrange("p (h a) -> p h a", a=1).to_broadcast([P, 8, 64])
                dve.tensor_tensor(xdt[:, g, tile, :].rearrange("p (h c) -> p h c", h=8),
                                  bank(3).rearrange("p (h c) -> p h c", h=8), d, ALU.mult).then_inc(*xdt_ready.one())

            def l_matrices(l, k):
                for hh in range(2):
                    dve.wait_ge(dec_ready.sem, dec_ready.at(l, 2 * k + hh + 1))
                    if hh == 0:
                        dve.wait_ge(cb_copied.sem, cb_copied.at(l, k // 4 + 1))
                    dve.tensor_tensor(dec[hh][:, :], dec[hh][:, :], cbt[:, :], ALU.mult).then_inc(*l_ready.one())

            def y_skip(l, k):
                dve.wait_ge(y_done.sem, y_done.at(l, k + 1))
                dve.scalar_tensor_tensor(out=xs[:, k, :], in0=xs[:, k, :], scalar=prm[:, C_DSK + k:C_DSK + k + 1],
                                         in1=bank(2, (k % 2) * SEQ, (k % 2 + 1) * SEQ), op0=ALU.mult, op1=ALU.add).then_inc(*ys_ready.one())

            def y_gate(l, i):
                dve.wait_ge(proj_read.sem, proj_read.at(l, N_Z - N_QK + i + 1))
                dve.wait_ge(ys_ready.sem, ys_ready.at(l, 16))
                dve.tensor_tensor(xs[:, 2 * i:2 * i + 2, :], xs[:, 2 * i:2 * i + 2, :],
                                  zs[i % 2][:, :].rearrange("p (c t) -> p c t", c=2), ALU.mult).then_inc(*yz_ready.one())

            def copy_pt(l, sl):
                dve.wait_ge(pt_done.sem, pt_done.at(l, sl + 1))
                if sl >= 1:
                    dve.wait_ge(pv_done.sem, pv_done.at(l, sl))
                dve.tensor_copy(pt[:, 1024:1152], bank(2, 256, 384)).then_inc(*pt_last.one())
                dve.tensor_copy(pt[:, 512:1024], bank(6)).then_inc(*pt_dve.one())

            def attn_out(l, sl):
                dve.wait_ge(pv_done.sem, pv_done.at(l, sl + 1))
                for tile in range(TILES):
                    ins = dve.tensor_scalar(att_tok[:, tile, sl * HEAD_DIM:(sl + 1) * HEAD_DIM],
                                            bank(7, tile * HEAD_DIM, (tile + 1) * HEAD_DIM), pinv[sl % 2][:, tile:tile + 1], None, ALU.mult)
                ins.then_inc(*att_tok_ready.one())

            def attn_lo(l):
                dve.wait_ge(att_hi.sem, att_hi.at(l, 1))
                dve.tensor_tensor(attL[:, :, :], att_turned_out, attH[:, :, :], ALU.subtract).then_inc(*att_lo.one())

            def softmax_max(l, sl):
                per_group = lambda t: t.rearrange("p (g k) -> p g k", g=GROUPS)
                mask = per_group(con[:, K_MASK:K_MASK + GROUPS * SEQ])
                dve.wait_ge(pro_dve, 1)
                dve.wait_ge(s_done.sem, s_done.at(l, sl + 1))
                dve.tensor_tensor_reduce(per_group(sm[:, 0:384]), per_group(bank(0, 0, 384)), mask[:, :, P:SEQ], 1.0, NEG, ALU.add, ALU.max,
                                         smax[:, 0:1]).then_inc(*smax_ready.one())
                dve.tensor_tensor_reduce(per_group(sm[:, 384:1152]), per_group(psm[:, 512:1280]), mask[:, :, :], 1.0, NEG, ALU.add, ALU.max,
                                         smax[:, 1:2]).then_inc(*smax_ready.one())
                dve.wait_ge(smax_ready.sem, smax_ready.at(l, 2 * sl + 2))
                dve.tensor_scalar(negm[:, :], smax[:, :], -SCALE, None, ALU.mult).then_inc(*negm_ready.one())

            def softmax_inv(l, sl):
                dve.wait_ge(p_exp.sem, p_exp.at(l, sl + 1))
                if sl >= 2:
                    dve.wait_ge(att_tok_ready.sem, att_tok_ready.at(l, sl - 1))
                dve.reciprocal(pinv[sl % 2][:, :], psum_[:, :]).then_inc(*p_inv.one())

            def y_norm(l, g):
                dve.wait_ge(yrstd.sem, yrstd.at(l, g + 1))
                for c in range(4 * g, 4 * g + 4):
                    ins = dve.scalar_tensor_tensor(out=xs[:, c, :], in0=xs[:, c, :], scalar=prm[:, C_SSM + c:C_SSM + c + 1],
                                                   in1=yrs[g % 2][:, :], op0=ALU.mult, op1=ALU.mult)
                ins.then_inc(*yn_ready.one())

            def y_lo(l, g):
                dve.wait_ge(yhi.sem, yhi.at(l, g + 1))
                dve.tensor_tensor(yL[:, g % 2, :, :], xs[:, 4 * g:4 * g + 4, :], yH[:, g % 2, :, :],
                                  ALU.subtract).then_inc(*ylo.one())

            def gate_att(l, a):
                s = SLOT_OF[(N_ATT + a) % 3]
                dve.wait_ge(used[s].sem, used[s].at(l, use_of(N_ATT + a) + 1))
                dve.wait_ge(proj_read.sem, proj_read.at(l, N_ATT - N_QK))
                for b in (2 * a, 2 * a + 1):
                    dve.tensor_tensor(gates[:, 2 * b:2 * b + 2, :], bank(4 + b).rearrange("p (c t) -> p c t", c=2),
                                      gates[:, 2 * b:2 * b + 2, :], ALU.mult).then_inc(*att_read.one())

            def merge(l, j):
                if j < 3:
                    dve.wait_ge(ssm_done.sem, ssm_done.at(l, j + 1))
                else:
                    n = N_OUT - 1
                    dve.wait_ge(used[SLOT_OF[n % 3]].sem, used[SLOT_OF[n % 3]].at(l, use_of(n) + 1))
                gs, ga = gates[:, 8 + 2 * j:10 + 2 * j, :], gates[:, 2 * j:2 * j + 2, :]
                dve.tensor_tensor(gs, bank(j).rearrange("p (c t) -> p c t", c=2), gs, ALU.mult).then_inc(*ssm_read.one())
                dve.wait_ge(ssm_read.sem, ssm_read.at(l, j + 1))
                dve.wait_ge(att_read.sem, att_read.at(l, j + 1))
                dve.tensor_tensor(ga, ga, gs, ALU.add).then_inc(*mix_ready.one())
                dve.wait_ge(mix_hi.sem, mix_hi.at(l, j + 1))
                dve.tensor_tensor(hL[:, 2 * j:2 * j + 2, :], ga, hH[:, 2 * j:2 * j + 2, :], ALU.subtract).then_inc(*mix_lo.one())

            def mixer(l):
                split_mix(l, 0)
                dve.wait_ge(dtw_hi.sem, dtw_hi.at(l, 1))
                dve.tensor_tensor(dtwL[:, :], dtw[:, :], dtwH[:, :], ALU.subtract).then_inc(*dtw_lo.one())
                residual(l, 0, 0.5)
                norm(l, 1, C_NM)
                d3 = lambda t: t[:, :].rearrange("p (t h) -> p t h", t=TILES)
                per_head = lambda t: t.rearrange("p (a h) -> p a h", a=1).to_broadcast([P, TILES, SSM_HEADS])
                dve.wait_ge(dt_done.sem, dt_done.at(l, 1))
                dve.tensor_tensor(d3(dts), bank(7, 0, 64).rearrange("p (t h) -> p t h", t=TILES),
                                  per_head(prm[:, C_DTB:C_DTB + 32]), ALU.add).then_inc(*dt_dve.one())
                dve.wait_ge(dt_dve.sem, dt_dve.at(l, 1))
                dve.tensor_scalar(dtm[:, :], dts[:, :], 0.0, None, ALU.max).then_inc(*dt_dve.one())
                for s in range(N_OUT):
                    if 0 <= s - 1 < N_QK:
                        taps(l, s - 1)
                    if s == 1:
                        dve.wait_ge(dt_act.sem, dt_act.at(l, 4))
                        dve.wait_ge(dt_dve.sem, dt_dve.at(l, 2))
                        dve.tensor_tensor(dt[:, :], dtm[:, :], dtl[:, :], ALU.add).then_inc(*dt_dve.one())
                        dve.wait_ge(dt_dve.sem, dt_dve.at(l, 3))
                        dve.scalar_tensor_tensor(out=d3(dta), in0=d3(dt), scalar=-1.0, in1=per_head(aexp[:, :]),
                                                 op0=ALU.mult, op1=ALU.mult).then_inc(*dt_dve.one())
                    if s == 3:
                        dve.wait_ge(cum_done.sem, cum_done.at(l, 1))
                        dve.wait_ge(dt_act.sem, dt_act.at(l, 5))
                        dve.tensor_scalar(ncum[:, :], bank(7, 320, 384), -1.0, None, ALU.mult).then_inc(*dt_dve.one())
                        dve.tensor_tensor(cumr[32:64, :], bank(7, 64, 320, 0, 32), cumr[0:32, :], ALU.subtract).then_inc(*dt_dve.one())
                    t = s - N_QK
                    if 0 <= t - 2 < 12:
                        qk_norm(l, t - 2)
                    if t >= 0 and t % 4 < 2 and t // 4 < SSM_GROUPS:
                        x_times_dt(l, t // 4, t % 4)
                    if 0 <= t - 1 < 16:
                        l_matrices(l, t - 1)
                    if 0 <= t - 2 < 16:
                        y_skip(l, t - 2)
                    if 0 <= t - 3 < 12:
                        rope(l, t - 3)
                    u = s - N_Z
                    if 0 <= u - 1 < 8:
                        y_gate(l, u - 1)
                    if 0 <= u - 1 < SLOTS:
                        copy_pt(l, u - 1)
                    if 0 <= u - 2 < SLOTS:
                        attn_out(l, u - 2)
                    if u == SLOTS + 3:
                        attn_lo(l)
                    if 0 <= u < SLOTS:
                        softmax_max(l, u)
                    w = s - N_G
                    if 0 <= w - 2 < 4:
                        y_norm(l, w - 2)
                    if s in Y_SPLIT:
                        y_lo(l, Y_SPLIT.index(s))
                    if s in (N_ATT + 1, N_ATT + 2):
                        gate_att(l, s - N_ATT - 1)
                    if s + 2 <= N_OUT:
                        split_mix(l, s + 2)
                    if 0 <= u < SLOTS:
                        softmax_inv(l, u)
                for j in range(4):
                    merge(l, j)
                for n in range(N_OUT + 1, N_MIX):
                    split_mix(l, n)

            with dve.Fori(0, DEPTH) as l:
                dve.tensor_copy(prm[:, :], prm_all[:, bass.ds(l * NPRM, NPRM)]).then_inc(*prm_ready.one())
                dve.wait_ge(prm_ready.sem, prm_ready.at(l, 1))
                ffn(l, 0)
                mixer(l)
                ffn(l, 1)
                residual(l, 2, 0.5)
            for t in range(TILES):
                dve.wait_ge(fin_pe, t + 1)
                dve.tensor_copy(v_flat[:, t * D_MODEL:(t + 1) * D_MODEL], psm[:, 1024 * t:1024 * t + 1024]).then_inc(fin_dve, 1)

        @block.tensor
        def _(pe):
            for s in range(3):
                pe.sem_inc(used[s].sem, 1)
            pe.wait_ge(ld_con, 32)
            pe.wait_ge(ld_prm, 16 * 12)
            for l in range(DEPTH):
                pe.transpose(bank(4, l * 120, l * 120 + 120), rows_a[:, l, :], ident[0:ROWS_A, 0:ROWS_A])
                pe.transpose(bank(4, 240 + l * 56, 296 + l * 56), rows_b[:, l, :], ident[0:ROWS_B, 0:ROWS_B])
                pe.matmul(bank(5, l * 96, l * 96 + 96), ones[0:1, :], row_r[0:1, l * NROW:l * NROW + 96], start=True, stop=True)
                for j in range(4):
                    for h in range(4):
                        c = l * NROW + 96 + 32 * j
                        ins = pe.matmul(bank(5, 192 + 4 * l + j, 193 + 4 * l + j, 32 * h, 32 * h + 32),
                                        row_r[0:1, c:c + 32], ones[0:1, 0:1], start=True, stop=True)
            ins.then_inc(pro_pe, 1)
            pe.wait_ge(ld_x, 16)
            for j in range(4):
                for c in (2 * j, 2 * j + 1):
                    for t in range(TILES):
                        ins = pe.transpose(bank(j, (c % 2) * SEQ + t * P, (c % 2) * SEQ + t * P + P),
                                           v_flat[:, t * D_MODEL + c * P:t * D_MODEL + (c + 1) * P], ident)
                ins.then_inc(pro_pe, 1)

            def split_ready(l, s, use):
                pe.wait_ge(hi_ready[s].sem, hi_ready[s].at(l, use + 1))
                pe.wait_ge(lo_ready[s].sem, lo_ready[s].at(l, use + 1))

            def product(o, wh, wl, xh, xl, first, last, shared=False):
                pe.matmul(o, wh, xh, start=first, stop=False, skip_group_check=shared)
                pe.matmul(o, wh, xl, start=False, stop=False, skip_group_check=shared)
                return pe.matmul(o, wl, xh, start=False, stop=last, skip_group_check=shared)

            def panel(s, b, ready=None):
                for c in range(2):
                    for k in range(KT):
                        if c == 0 and ready is not None:
                            ready(k)
                        w0 = k * PC + c * P
                        ins = product(bank(b, c * SEQ, (c + 1) * SEQ), wH[s][:, w0:w0 + P], wL[s][:, w0:w0 + P],
                                      hH[:, k, :], hL[:, k, :], k == 0, k == KT - 1)
                return ins

            def norm_sum(l, k):
                for j in range(4):
                    pe.wait_ge(sq_ready.sem, sq_ready.at(l, 4 * k + j + 1))
                    for c in range(2):
                        ins = pe.matmul(bank(6, 0, SEQ), ones, sq[:, j, c * SEQ:(c + 1) * SEQ], start=(j == 0 and c == 0),
                                        stop=(j == 3 and c == 1))
                ins.then_inc(*ss_done.one())

            def h_ready(l, k):
                def wait(kt):
                    if kt % 2 == 0:
                        pe.wait_ge(hlo.sem, hlo.at(l, 4 * k + kt // 2 + 1))
                return wait

            def ffn(l, f):
                use0, e0 = (0, USES - FI)[f], f * FI

                def gate(i, times=1, ready=None):
                    split_ready(l, GATE_SLOT, use0 + i)
                    panel(GATE_SLOT, 4, ready).then_inc(*used[GATE_SLOT].one(times))

                def up(i, times=1):
                    split_ready(l, UP_SLOT, use0 + i)
                    panel(UP_SLOT, 5).then_inc(*used[UP_SLOT].one(times))

                def down(i, times=1, first=False, last=False):
                    split_ready(l, DOWN_SLOT, use0 + i)
                    pe.wait_ge(hidlo.sem, hidlo.at(l, e0 + i + 1))
                    for c in range(KT):
                        for k in range(2):
                            w0 = k * D_MODEL + c * P
                            ins = product(bank(c // 2, (c % 2) * SEQ, (c % 2 + 1) * SEQ),
                                          wH[DOWN_SLOT][:, w0:w0 + P], wL[DOWN_SLOT][:, w0:w0 + P],
                                          hidH[:, k * SEQ:(k + 1) * SEQ], hidL[:, k * SEQ:(k + 1) * SEQ],
                                          first and c % 2 == 0 and k == 0, last and k == 1, shared=True)
                        if last and c in (1, 3, 5):
                            ins.then_inc(*acc_done.one())
                    ins.then_inc(*used[DOWN_SLOT].one(times))

                norm_sum(l, 2 * f)
                gate(0, ready=h_ready(l, 2 * f))
                up(0)
                pe.wait_ge(silu_done.sem, silu_done.at(l, e0 + 1))
                gate(1)
                down(0, first=True)
                up(1)
                with pe.Fori(2, FI) as i:
                    pe.wait_ge(silu_done.sem, silu_done.at(l, e0 + i))
                    gate(i, FI - 2)
                    down(i - 1, FI - 2)
                    up(i, FI - 2)
                down(FI - 1, last=True)

            def dt_product(l):
                pe.wait_ge(dtw_lo.sem, dtw_lo.at(l, 1))
                ready = h_ready(l, 1)
                for t in range(TILES):
                    for k in range(KT):
                        if t == 0:
                            ready(k)
                        c = k * SSM_HEADS
                        ins = product(bank(7, 32 * t, 32 * t + 32), hH[:, k, t * P:(t + 1) * P], hL[:, k, t * P:(t + 1) * P],
                                      dtwH[:, c:c + 32], dtwL[:, c:c + 32], k == 0, k == KT - 1)
                ins.then_inc(*dt_done.one())

            def cumulate(l):
                pe.wait_ge(dt_dve.sem, dt_dve.at(l, 4))
                pe.matmul(bank(7, 64, 320, 0, 32), dta[:, 0:32], tri, start=True, stop=False)
                pe.matmul(bank(7, 192, 320, 0, 32), dta[:, 32:64], tri[:, 0:P], start=False, stop=True)
                pe.matmul(bank(7, 320, 352), tri[:, 0:P], dta[:, 0:32], start=True, stop=True)
                pe.matmul(bank(7, 352, 384), ones, dta[:, 0:32], start=True, stop=False)
                pe.matmul(bank(7, 352, 384), tri[:, 0:P], dta[:, 32:64], start=False, stop=True).then_inc(*cum_done.one())

            def qk_sum(l, i):
                pe.wait_ge(qsq_added.sem, qsq_added.at(l, i + 1))
                if i >= 1:
                    pe.wait_ge(qk_ln.sem, qk_ln.at(l, i))
                o = bank(6, (i % 2) * SEQ, (i % 2 + 1) * SEQ)
                blk = con[:, K_BLK:K_BLK + P]
                pe.matmul(o, blk, qsq[i % 2][:, 0:SEQ], start=True, stop=True).then_inc(*qk_ss.one())

            def x_transpose(l, g, tile):
                pe.wait_ge(conv_silu.sem, conv_silu.at(l, 6 + 2 * g))
                if g or tile:
                    pe.wait_ge(xdt_ready.sem, xdt_ready.at(l, 2 * g + tile))
                for c in range(4):
                    ins = pe.transpose(bank(3, c * P, (c + 1) * P), xs[:, 4 * g + c, tile * P:(tile + 1) * P], ident)
                ins.then_inc(*xt_done.one())

            def cb(l, g):
                if g == 0:
                    pe.wait_ge(dt_dve.sem, dt_dve.at(l, 6))
                else:
                    pe.wait_ge(cb_copied.sem, cb_copied.at(l, g))
                pe.matmul(bank(7, 0, 256), bc[:, g, 0:P], bc[:, 4 + g, :], start=True, stop=True)
                pe.matmul(bank(7, 256, 384), bc[:, g, P:SEQ], bc[:, 4 + g, P:SEQ], start=True, stop=True).then_inc(*cb_done.one())

            def decay_sums(l, k):
                for hh in range(2):
                    head = 2 * k + hh
                    if k == 0:
                        pe.wait_ge(dt_dve.sem, dt_dve.at(l, 6))
                        pe.wait_ge(con_ready, 1)
                    else:
                        pe.wait_ge(dec_ready.sem, dec_ready.at(l, head - 1))
                    sel = sel_r[0:64, head:head + 1].to_broadcast([64, P])
                    pe.matmul(bank(hh, 0, 256), sel, cumr[:, :], start=True, stop=False)
                    pe.matmul(bank(hh, 0, 128), ident_r, neg_r, start=False, stop=True)
                    pe.matmul(bank(hh, 256, 384), sel, cumr[:, P:SEQ], start=True, stop=False)
                    pe.matmul(bank(hh, 256, 384), ident_r, neg_r, start=False, stop=True).then_inc(*decay_sum.one())

            def ssd(l, k):
                g, c0 = k // 4, (k % 4) * P
                pe.wait_ge(l_ready.sem, l_ready.at(l, 2 * k + 2))
                pe.wait_ge(xdt_ready.sem, xdt_ready.at(l, 2 * g + 2))
                if k >= 1:
                    pe.wait_ge(ys_ready.sem, ys_ready.at(l, k))
                b0 = (k % 2) * SEQ
                for hh in range(2):
                    r = 64 * hh
                    pe.matmul(bank(2, b0, b0 + SEQ, r, r + 64), xdt[:, g, 0, c0 + r:c0 + r + 64], dec[hh][:, 0:256], start=True, stop=False)
                    ins = pe.matmul(bank(2, b0 + P, b0 + SEQ, r, r + 64), xdt[:, g, 1, c0 + r:c0 + r + 64], dec[hh][:, 256:384],
                                    start=False, stop=True)
                ins.then_inc(*y_done.one())

            def scores(l, sl):
                if sl == 0:
                    pe.wait_ge(rope_ready.sem, rope_ready.at(l, 12))
                    pe.wait_ge(dec_ready.sem, dec_ready.at(l, 32))
                    pe.wait_ge(ys_ready.sem, ys_ready.at(l, 16))
                else:
                    pe.wait_ge(smax_ready.sem, smax_ready.at(l, 2 * sl))
                heads = [divmod(SLOTS * g + sl, 2) for g in range(GROUPS)]
                for g, (c, h) in enumerate(heads):
                    r = slice(64 * h, 64 * h + 64)
                    pe.matmul(bank(0, g * P, (g + 1) * P), qk[r, 0, c, 0:P], qk[r, 1, c, 0:P], start=True, stop=True)
                for g, (c, h) in enumerate(heads):
                    r = slice(64 * h, 64 * h + 64)
                    if g == 2 and sl >= 1:
                        pe.wait_ge(pt_last.sem, pt_last.at(l, sl))
                    ins = pe.matmul(psm[:, 512 + g * SEQ:512 + (g + 1) * SEQ], qk[r, 0, c, P:SEQ], qk[r, 1, c, :],
                                    start=True, stop=True)
                ins.then_inc(*s_done.one())

            def p_transpose(l, sl):
                pe.wait_ge(p_exp.sem, p_exp.at(l, sl + 1))
                if sl == 0:
                    pe.wait_ge(qk_ln.sem, qk_ln.at(l, 12))
                else:
                    pe.wait_ge(pt_act.sem, pt_act.at(l, sl))
                    pe.wait_ge(pt_dve.sem, pt_dve.at(l, sl))
                for i in range(9):
                    g, j = divmod(i, 3)
                    c = (g * P, 384 + g * SEQ, 384 + g * SEQ + P)[j]
                    o = bank(2, 256, 384) if i == 8 else bank((3, 6)[i // 4], (i % 4) * P, (i % 4 + 1) * P)
                    ins = pe.transpose(o, sm[:, c:c + P], ident)
                ins.then_inc(*pt_done.one())

            def p_times_v(l, sl):
                pe.wait_ge(pt_act.sem, pt_act.at(l, sl + 1))
                pe.wait_ge(pt_dve.sem, pt_dve.at(l, sl + 1))
                pe.wait_ge(proj_read.sem, proj_read.at(l, N_Z - N_QK))
                if sl >= 1:
                    pe.wait_ge(att_tok_ready.sem, att_tok_ready.at(l, sl))
                for tile in range(TILES):
                    o = bank(7, tile * HEAD_DIM, (tile + 1) * HEAD_DIM)
                    blocks = [(g, key) for g in range(GROUPS) for key in range(tile + 1)]
                    for g, key in blocks:
                        c, j = g * ATT_DIM + sl * HEAD_DIM, 3 * g + tile + key
                        ins = pe.matmul(o, pt[:, j * P:(j + 1) * P], v[:, key, c:c + HEAD_DIM],
                                        start=((g, key) == blocks[0]), stop=((g, key) == blocks[-1]))
                ins.then_inc(*pv_done.one())

            def att_transpose(l):
                pe.wait_ge(att_tok_ready.sem, att_tok_ready.at(l, SLOTS))
                for c in range(4):
                    for tile in range(TILES):
                        o = c * SEQ + tile * P
                        ins = pe.transpose(psm[:, 1024 + o:1024 + o + P], att_tok[:, tile, c * P:(c + 1) * P], ident)
                ins.then_inc(*att_turned.one())

            def y_sum(l, g):
                pe.wait_ge(ysq_added.sem, ysq_added.at(l, 2 * g + 2))
                if g < 2:
                    pe.wait_ge(smax_ready.sem, smax_ready.at(l, 16))
                else:
                    pe.wait_ge(ysln.sem, ysln.at(l, g - 1))
                pe.matmul(bank(g % 2, 0, SEQ), ones, sq[:, 2 * (g % 2), 0:SEQ], start=True, stop=True).then_inc(*yss_done.one())

            def bank_free(l, n):
                m = n - 2
                if 0 <= m < N_QK:
                    pe.wait_ge(conv_tap.sem, conv_tap.at(l, 6 * m + 6))
                elif m >= N_QK:
                    pe.wait_ge(proj_read.sem, proj_read.at(l, m - N_QK + 1))

            def ssm_chunk(m, c):
                s, g = SLOT_OF[(N_SSM + m) % 3], m // 2
                for k in range(2):
                    w0, y = k * D_MODEL + c * P, 2 * (m % 2) + k
                    ins = product(bank(c // 2, (c % 2) * SEQ, (c % 2 + 1) * SEQ), wH[s][:, w0:w0 + P], wL[s][:, w0:w0 + P],
                                  yH[:, g % 2, y, :], yL[:, g % 2, y, :], m == 0 and c % 2 == 0 and k == 0,
                                  m == 7 and k == 1, shared=True)
                return ins

            def mixer(l):
                norm_sum(l, 1)
                dt_product(l)
                for n in range(N_ATT):
                    if n == 2:
                        cumulate(l)
                    t = n - N_QK
                    if 0 <= t - 2 < 12:
                        qk_sum(l, t - 2)
                    if t >= 0 and t % 4 < 2 and t // 4 < SSM_GROUPS:
                        x_transpose(l, t // 4, t % 4)
                    if t >= 0 and t % 4 == 0 and t // 4 < SSM_GROUPS:
                        cb(l, t // 4)
                    if 0 <= t - 1 < 16:
                        decay_sums(l, t - 1)
                    if 0 <= t - 2 < 16:
                        ssd(l, t - 2)
                    u = n - N_Z
                    if 0 <= u - 2 < SLOTS:
                        p_times_v(l, u - 2)
                    if 0 <= u - 1 < SLOTS:
                        p_transpose(l, u - 1)
                    if 0 <= u < SLOTS:
                        scores(l, u)
                    if u == SLOTS + 2:
                        att_transpose(l)
                    w = n - N_G
                    if 0 <= w - 2 < 4:
                        y_sum(l, w - 2)
                    s, b = SLOT_OF[n % 3], 4 + n % 2
                    bank_free(l, n)
                    split_ready(l, s, use_of(n))
                    if N_V <= n < N_Z:
                        for tile in range(TILES):
                            for k in range(KT):
                                ts = slice(tile * P, (tile + 1) * P)
                                ins = product(bank(b, tile * PC, (tile + 1) * PC), hH[:, k, ts], hL[:, k, ts],
                                              wH[s][:, k * PC:(k + 1) * PC], wL[s][:, k * PC:(k + 1) * PC], k == 0, k == KT - 1)
                    else:
                        ins = panel(s, b)
                    ins.then_inc(*used[s].one())
                for a in range(2):
                    n = N_ATT + a
                    s = SLOT_OF[n % 3]
                    split_ready(l, s, use_of(n))
                    if a == 0:
                        pe.wait_ge(att_lo.sem, att_lo.at(l, 1))
                        pe.wait_ge(proj_read.sem, proj_read.at(l, N_ATT - N_QK))
                    for c in range(4):
                        for k in range(4):
                            w0 = k * 512 + c * P
                            ins = product(bank(4 + 2 * a + c // 2, (c % 2) * SEQ, (c % 2 + 1) * SEQ), wH[s][:, w0:w0 + P], wL[s][:, w0:w0 + P],
                                          attH[:, k, :], attL[:, k, :], k == 0, k == 3)
                    ins.then_inc(*used[s].one())
                for m in range(6):
                    n, g = N_SSM + m, m // 2
                    s = SLOT_OF[n % 3]
                    split_ready(l, s, use_of(n))
                    pe.wait_ge(ylo.sem, ylo.at(l, g + 1))
                    if m == 0:
                        pe.wait_ge(ysln.sem, ysln.at(l, 4))
                    for c in range(KT):
                        ins = ssm_chunk(m, c)
                    ins.then_inc(*used[s].one())
                last = [SLOT_OF[(N_SSM + m) % 3] for m in (6, 7)]
                for m, s in zip((6, 7), last):
                    split_ready(l, s, use_of(N_SSM + m))
                pe.wait_ge(ylo.sem, ylo.at(l, 4))
                for c in range(KT):
                    ins = ssm_chunk(6, c)
                    if c == KT - 1:
                        ins.then_inc(*used[last[0]].one())
                    ins = ssm_chunk(7, c)
                    if c in (1, 3, 5):
                        ins.then_inc(*ssm_done.one())
                ins.then_inc(*used[last[1]].one())
                for j in range(4):
                    n = N_OUT + j
                    s = SLOT_OF[n % 3]
                    split_ready(l, s, use_of(n))
                    if j == 0:
                        pe.wait_ge(att_read.sem, att_read.at(l, 4))

                    def mixed(k):
                        if k % 2 == 0:
                            pe.wait_ge(mix_lo.sem, mix_lo.at(l, k // 2 + 1))
                    ins = panel(s, j, mixed if j == 0 else None)
                    ins.then_inc(*used[s].one())

            with pe.Fori(0, DEPTH) as l:
                ffn(l, 0)
                mixer(l)
                ffn(l, 1)
            pe.wait_ge(x_ready.sem, 12 * DEPTH + 4)
            for t in range(TILES):
                for c in range(KT):
                    ins = pe.transpose(psm[:, 1024 * t + c * P:1024 * t + (c + 1) * P], xT[:, c, t * P:(t + 1) * P], ident)
                ins.then_inc(fin_pe, 1)

    for s in signals:
        if s.unit == 1:
            assert s.seen == s.per_layer, (s.sem, s.seen, s.per_layer)


_INS = ['x', 'ffn1_norm_w', 'ffn1_w_gate', 'ffn1_w_up', 'ffn1_w_down', 'mix_norm_w', 'w_in', 'b_gates', 'q_norm_w', 'k_norm_w',
        'conv_w', 'conv_b', 'dt_bias', 'a_log', 'd_skip', 'ssm_norm_w', 'w_att_proj', 'w_ssm_proj', 'w_out', 'ffn2_norm_w',
        'ffn2_w_gate', 'ffn2_w_up', 'ffn2_w_down']


def kernel(**inputs):
    import concourse.bacc as _bacc
    from concourse.bass_utils import run_bass_kernel_spmd as _run

    nc = _bacc.Bacc("TRN2", target_bir_lowering=False, num_devices=1)
    arrays, args = {}, []
    for name in _INS:
        arrays[f"in_{name}"] = np.ascontiguousarray(inputs[name])
    arrays["in_constants"] = constants()
    for name, a in arrays.items():
        args.append(nc.dram_tensor(name, a.shape, mybir.dt.from_np(a.dtype), kind="ExternalInput").ap())
    out = nc.dram_tensor("out_0", (1, SEQ, D_MODEL), F32, kind="ExternalOutput").ap()
    program(nc, *args, out)
    r = _run(nc, [arrays], core_ids=[0])
    return r.results[0]["out_0"]
```

```python
from contextlib import ExitStack

import numpy as np
import concourse.bass as bass
from concourse import mybir

F32 = mybir.dt.float32
F32R = mybir.dt.float32r
ALU = mybir.AluOpType
ACT = mybir.ActivationFunctionType
LN_EXP = "natural_log_exp_and_others"

P = 128
SEQ = 256
TILES = SEQ // P
DEPTH = 2
D_MODEL = 1024
KT = D_MODEL // P
D_FF = 2816
EPS = 1e-6
HEAD_DIM = 64
HALF = HEAD_DIM // 2
GROUPS = 3
SLOTS = 8
N_ATT_HEADS = GROUPS * SLOTS
QKV = N_ATT_HEADS * HEAD_DIM
ATT_DIM = SLOTS * HEAD_DIM
D_INNER = 2 * D_MODEL
SSM_HEADS = D_INNER // 64
SSM_GROUPS = 4
STATE = 128
TAPS = 4
XBC = D_INNER + 2 * SSM_GROUPS * STATE
N_IN = 3 * QKV + D_INNER + XBC + SSM_HEADS + 2 * D_MODEL
SCALE = HEAD_DIM ** -0.5
NEG = -1.0e30

PC = 256
PE_LEN = KT * PC
FI = D_FF // PC
Q_AT, K_AT, V_AT = 0, QKV, 2 * QKV
Z_AT = 3 * QKV
XBC_AT = Z_AT + D_INNER
DT_AT = XBC_AT + XBC
GATE_AT = DT_AT + SSM_HEADS
XBC_P = [8, 9, 10, 11] + list(range(8))
COLS = ([XBC_AT + PC * i for i in XBC_P] + [Q_AT + PC * i for i in range(6)] + [K_AT + PC * i for i in range(6)]
        + [V_AT + PC * i for i in range(6)] + [Z_AT + PC * i for i in range(8)] + [GATE_AT + PC * i for i in range(8)])
N_XBC = 0
N_QK = len(XBC_P)
N_V = N_QK + 12
N_Z = N_V + 6
N_G = N_Z + 8
N_ATT = N_G + 8
N_SSM = N_ATT + 2
N_OUT = N_SSM + 8
N_MIX = N_OUT + 4
Y_SUMS = (2, 5)
Y_SPLIT = (N_G + 3, N_G + 4, N_SSM + 2, N_SSM + 4)
SLOT_OF = (0, 2, 1)
GATE_SLOT, DOWN_SLOT, UP_SLOT = 0, 1, 2
USES = 2 * FI + N_MIX // 3

C_CONVW, C_CONVB, C_N1, C_NM, C_N2, C_SSM, C_BG, C_DSK = 0, 96, 120, 128, 136, 144, 160, 176
C_DTB, C_ALOG, C_QK = 192, 224, 256
NPRM = 260
ROWS_A, ROWS_B = 120, 56
NROW = 3 * SSM_HEADS + 2 * HEAD_DIM

K_ID, K_BLK, K_TRI, K_ONE, K_MASK, K_CS, K_SEL = 0, 128, 256, 384, 512, 1280, 1792
NKEPT = K_SEL
NEARLY = K_MASK
NCONST = K_SEL + SSM_HEADS


def constants():
    c = np.zeros((P, NCONST), np.float32)
    p = np.arange(P)
    c[:, K_ID:K_ID + P] = np.eye(P)
    c[:, K_ONE:K_ONE + P] = 1.0
    c[:, K_BLK:K_BLK + P] = (p[:, None] // HALF == p[None, :] // HALF)
    c[:, K_TRI:K_TRI + P] = (p[:, None] <= p[None, :])
    for g, (window, dil) in enumerate(((128, 1), (512, 4), (2048, 16))):
        q = np.arange(P, SEQ)[:, None]
        k = np.arange(SEQ)[None, :]
        ok = (k <= q) & (q - k <= window) & ((q - k) % dil == 0)
        c[:, K_MASK + g * SEQ:K_MASK + (g + 1) * SEQ] = np.where(ok, 0.0, NEG)
    inv = (1.0 / (np.float32(10000.0) ** (np.arange(0, HEAD_DIM, 2, dtype=np.float32) / np.float32(HEAD_DIM)))).astype(np.float32)
    ang = (np.arange(SEQ, dtype=np.float32)[None, :] * inv[:, None]).astype(np.float32).astype(np.float64)
    c[:, K_CS:K_CS + SEQ] = np.tile(np.cos(ang), (4, 1))
    c[:, K_CS + SEQ:K_CS + 2 * SEQ] = np.tile(np.sin(ang), (4, 1))
    c[:2 * SSM_HEADS, K_SEL:K_SEL + SSM_HEADS] = np.tile(np.eye(SSM_HEADS), (2, 1))
    return c


class Signal:

    def __init__(self, sem, per_layer, before=0, unit=1):
        self.sem, self.per_layer, self.before, self.unit, self.seen = sem, per_layer, before, unit, 0

    def at(self, layer, count):
        return layer * (self.per_layer * self.unit) + (self.before + count) * self.unit

    def one(self, times=1):
        self.seen += times
        return self.sem, self.unit


def halves_in(tile, f):
    return tile[:, :].rearrange("p (kh f c) -> p kh f c", f=2, c=HALF)[:, :, f, :].rearrange("p (k h) c -> p k h c", h=4)


def halves_out(tile, f):
    return tile[:, :].rearrange("p (k f h c) -> p k f h c", f=2, h=4, c=HALF)[:, :, f, :, :]


def program(nc, x, n1w, w1g, w1u, w1d, nmw, w_in, b_gates, q_norm, k_norm, conv_w, conv_b, dt_bias, a_log,
            d_skip, ssm_w, w_att, w_ssm, w_out, n2w, w2g, w2u, w2d, consts, out):
    with ExitStack() as ctx:
        def sb(name, shape, dt=F32):
            return ctx.enter_context(nc.sbuf_tensor(name, shape, dt))

        signals = []

        def signal(name, per_layer, before=0, unit=1):
            s = Signal(ctx.enter_context(nc.semaphore(name)), per_layer, before, unit)
            signals.append(s)
            return s

        con = sb("con", [P, NKEPT])
        con_r = sb("con_r", [P, SSM_HEADS], F32R)
        xT = sb("xT", [P, KT, SEQ])
        hH, hL = sb("hH", [P, KT, SEQ], F32R), sb("hL", [P, KT, SEQ], F32R)
        raw = [sb(f"raw{s}", [P, PE_LEN]) for s in range(3)]
        wH = [sb(f"wH{s}", [P, PE_LEN], F32R) for s in range(3)]
        wL = [sb(f"wL{s}", [P, PE_LEN], F32R) for s in range(3)]
        sq = sb("sq", [P, 4, 512])
        prm_all = sb("prm_all", [P, DEPTH * NPRM])
        prm = sb("prm", [P, NPRM])
        qk = sb("qk", [P, 2, N_ATT_HEADS // 2, SEQ])
        gates = qk[:, :, :, :].rearrange("p a b t -> p (a b) t")
        v = sb("v", [P, TILES, QKV])
        v_flat = v[:, :, :].rearrange("p t n -> p (t n)")
        ht = v_flat[:, 0:KT * SEQ].rearrange("p (k t) -> p k t", k=KT)
        dtw = v_flat[:, 2560:2560 + KT * SSM_HEADS]
        xs = sb("xs", [P, 16, SEQ])
        rows_a = xs[0:ROWS_A, 0:1, :].rearrange("p a (l c) -> p (a l) c", l=DEPTH)
        rows_b = xs[0:ROWS_B, 1:2, :].rearrange("p a (l c) -> p (a l) c", l=DEPTH)
        con_tail = xs[:, 4, 0:NCONST - NKEPT]
        row_r = xs[0:1, 2:4, :].rearrange("p a t -> p (a t)")[:, 0:DEPTH * NROW]
        with (nc.sbuf_tensor("bc", [P, 8, SEQ], F32) as bc,
              nc.sbuf_tensor("qraw", [P, 2, 512], F32) as qraw2, nc.sbuf_tensor("qn", [P, 2, 2, SEQ], F32) as qn2):
            pass
        attH, attL = sb("attH", [P, 4, SEQ], F32R), sb("attL", [P, 4, SEQ], F32R)
        sb("rest", [P, 2048])
        hidH, hidL = (t[:, 0:2, :].rearrange("p a t -> p (a t)") for t in (attH, attL))
        dtwH, dtwL = attH[:, 2, :], attL[:, 2, :]
        with nc.sbuf_tensor("xdt", [P, SSM_GROUPS, TILES, 512], F32) as xdt:
            pass
        yH, yL = sb("yH", [P, 2, 4, SEQ], F32R), sb("yL", [P, 2, 4, SEQ], F32R)
        acc = [sq[:, i, :] for i in range(2)]
        zs = acc
        qraw, qn = [qraw2[:, i, :] for i in range(2)], [qn2[:, i, :, :] for i in range(2)]
        qsq = [sq[:, i, :] for i in range(2)]
        qrs2 = sb("qrs", [P, 2, SEQ])
        qrs = [qrs2[:, i, :] for i in range(2)]
        rstd = qrs[0]
        ropa, ropb = (sq[:, i, :].rearrange("p (a t) -> p a t", a=2) for i in (2, 3))
        dtu, dte, dtl, dtm = (qrs[1][:, 64 * i:64 * i + 64] for i in range(4))
        dt, cumk = (sb(n, [P, 64]) for n in ("dt", "cumk"))
        cumr = sb("cumr", [2 * SSM_HEADS, SEQ], F32R)
        cbt = sb("cbt", [P, 384])
        dec = sb("dec", [P, 2, 384])
        scratch = xdt[:, :, :, :].rearrange("p g t n -> p (g t n)")
        sm, pt = scratch[:, 0:1152], scratch[:, 1152:2304]
        att_tok = scratch[:, 2304:3328].rearrange("p (t n) -> p t n", t=TILES)
        dth = scratch[0:SSM_HEADS, 2048:2048 + SEQ]
        dts, dta, aexp = scratch[:, 1152:1216], scratch[:, 1216:1280], scratch[:, 1280:1312]
        sg, hid = scratch[:, 0:512], scratch[:, 512:1024]
        small = sb("small", [P, 16])
        smax, negm, psum_ = (small[:, 2 * i:2 * i + 2] for i in range(3))
        pinv = [small[:, 6 + 2 * i:8 + 2 * i] for i in range(2)]
        eps = small[:, 10:11]
        yrs = qrs
        psm = ctx.enter_context(nc.psum_tensor("psm", [P, 8 * 512], F32))

        y_sums = psm[:, 0:1024].rearrange("p (b n) -> p b n", b=2)[:, :, 0:SEQ]
        att_turned_out = psm[:, 1024:2048].rearrange("p (c t) -> p c t", t=SEQ)

        def bank(b, lo=0, hi=512, p0=0, p1=P):
            return psm[p0:p1, b * 512 + lo:b * 512 + hi]

        ident = con[:, K_ID:K_ID + P]
        ones = con[:, K_ONE:K_ONE + P]
        tri = con[:, K_TRI:K_TRI + SEQ]
        sel_r = con_r

        raw_full = [signal(f"raw_full{s}", USES, unit=16) for s in range(3)]
        hi_ready = [signal(f"hi_ready{s}", USES) for s in range(3)]
        lo_ready = [signal(f"lo_ready{s}", USES, 1) for s in range(3)]
        used = [signal(f"panel_used{s}", USES, 1) for s in range(3)]
        x_ready = signal("x_ready", 12, 0)
        sq_ready, ss_done = signal("sq_ready", 12), signal("ss_done", 3)
        ln_done, rstd_ready = signal("ln_done", 3), signal("rstd_ready", 3)
        sq_added = signal("sq_added", 6)
        hn_ready, hhi = signal("hn_ready", 24), signal("hhi", 24)
        mix_passed = signal("mix_passed", KT - 1)
        hlo = [signal("hlo_even", 12), signal("hlo_odd", 12)]
        acc_done = signal("acc_done", 6)
        silu_done, hid_ready = signal("silu_done", 2 * FI), signal("hid_ready", 2 * FI + 2)
        gate_scaled, silu_scaled = signal("gate_scaled", 2 * FI), signal("silu_scaled", 2 * FI)
        hidhi, hidlo, up_part = signal("hidhi", 2 * FI + 2), signal("hidlo", 2 * FI + 2), signal("up_part", 2)
        prm_ready = signal("prm_ready", 1)
        dtw_full, dtw_hi, dtw_lo = signal("dtw_full", 1, 0, 16), signal("dtw_hi", 1), signal("dtw_lo", 1, 1)
        dt_copied, dt_turned = signal("dt_copied", 1), signal("dt_turned", 1)
        dt_done, cum_done = signal("dt_done", 1), signal("cum_done", 1)
        dt_dve, dt_act = signal("dt_dve", 6), signal("dt_act", 5)
        conv_bias, conv_tap, conv_silu = signal("conv_bias", 24), signal("conv_tap", 72), signal("conv_silu", 12)
        proj_read = signal("proj_read", N_ATT - N_QK)
        qk_ss, qk_ln, qk_rstd = signal("qk_ss", 12), signal("qk_ln", 12), signal("qk_rstd", 12)
        qn_ready, rope_ab, rope_ready = signal("qn_ready", 12), signal("rope_ab", 12), signal("rope_ready", 12)
        xt_done, xdt_ready = signal("xt_done", 8), signal("xdt_ready", 8)
        cb_done, cb_copied = signal("cb_done", 4), signal("cb_copied", 4)
        decay_sum, dec_ready, l_ready = signal("decay_sum", 16), signal("dec_ready", 16), signal("l_ready", 16)
        dec_diff = signal("dec_diff", 16)
        y_done, ys_ready = signal("y_done", 16), signal("ys_ready", 16)
        s_done, smax_ready, negm_ready = signal("s_done", 8), signal("smax_ready", 16), signal("negm_ready", 8)
        p_exp, p_inv = signal("p_exp", 8), signal("p_inv", 8)
        pt_done, pt_act, pt_dve = signal("pt_done", 8), signal("pt_act", 8), signal("pt_dve", 8)
        pt_last = signal("pt_last", 8)
        pv_done, att_tok_ready, att_turned = signal("pv_done", 8), signal("att_tok_ready", 8), signal("att_turned", 1)
        att_hi, att_lo = signal("att_hi", 1), signal("att_lo", 1)
        qsq_added, ysq_added = signal("qsq_added", 12), signal("ysq_added", 8)
        yz_ready, ysq_ready, yss_done = signal("yz_ready", 8), signal("ysq_ready", 4), signal("yss_done", 4)
        ysln, yrstd, yn_ready = signal("ysln", 2), signal("yrstd", 2), signal("yn_ready", 4)
        yhi, ylo = signal("yhi", 4), signal("ylo", 4)
        att_read, ssm_done, ssm_read = signal("att_read", 4), signal("ssm_done", 3), signal("ssm_read", 4)
        mix_ready, mix_hi, mix_lo = signal("mix_ready", 4), signal("mix_hi", 4), signal("mix_lo", 4)
        ld_con, ld_x, ld_prm, ld_sel, ld_rest = (ctx.enter_context(nc.semaphore(n))
                                                 for n in ("ld_con", "ld_x", "ld_prm", "ld_sel", "ld_rest"))
        con_ready, pro_pe, pro_dve = (ctx.enter_context(nc.semaphore(n)) for n in ("con_ready", "pro_pe", "pro_dve"))
        fin_pe, fin_dve, stored = (ctx.enter_context(nc.semaphore(n)) for n in ("fin_pe", "fin_dve", "stored"))

        sp_turn = ctx.enter_context(nc.semaphore("sp_turn"))

        def use_of(n):
            return FI + n // 3

        block = ctx.enter_context(nc.Block())

        @block.sync
        def _(sp):
            sp.dma_start(con[:, 0:NEARLY], consts[:, 0:NEARLY]).then_inc(ld_con, 16)
            for src, tile, r0, r1 in (
                    (conv_w.rearrange("l k (c p) -> (k c) l p", p=P), rows_a, 0, 96),
                    (conv_b.rearrange("l (c p) -> c l p", p=P), rows_a, 96, 120),
                    (n1w.rearrange("l (c p) -> c l p", p=P), rows_b, 0, 8),
                    (nmw.rearrange("l (c p) -> c l p", p=P), rows_b, 8, 16),
                    (n2w.rearrange("l (c p) -> c l p", p=P), rows_b, 16, 24)):
                sp.dma_start(tile[r0:r1, :, :], src).then_inc(ld_prm, 16)

            flat = {id(w): w.rearrange("l r n -> (l r) n") for w in (w1g, w1u, w1d, w2g, w2u, w2d, w_in, w_att, w_ssm, w_out)}

            def load(l, slot, use, w, rows, row0, nrows, col0, ncols):
                sp.wait_ge(lo_ready[slot].sem, lo_ready[slot].at(l, use))
                sp.sem_inc(sp_turn, 1)
                src = flat[id(w)][bass.ds(l * rows + row0, nrows), bass.ds(col0, ncols)]
                sp.dma_start(raw[slot][:, :].rearrange("p (k n) -> p k n", n=ncols),
                             src.rearrange("(k p) n -> p k n", p=P)).then_inc(raw_full[slot].sem, 16)

            def ffn(l, use0, wg, wu, wd):
                def gate(i):
                    load(l, GATE_SLOT, use0 + i, wg, D_MODEL, 0, D_MODEL, i * PC, PC)

                def up(i):
                    load(l, UP_SLOT, use0 + i, wu, D_MODEL, 0, D_MODEL, i * PC, PC)

                def down(i):
                    load(l, DOWN_SLOT, use0 + i, wd, D_FF, i * PC, PC, 0, D_MODEL)

                gate(0)
                up(0)
                with sp.Fori(1, FI) as i:
                    gate(i)
                    down(i - 1)
                    up(i)
                down(FI - 1)

            with sp.Fori(0, DEPTH) as l:
                sp.wait_ge(dtw_lo.sem, dtw_lo.at(l, 0))
                sp.sem_inc(sp_turn, 1)
                sp.dma_start(dtw[:, :].rearrange("p (k n) -> p k n", n=SSM_HEADS),
                             flat[id(w_in)][bass.ds(l * D_MODEL, D_MODEL), DT_AT:DT_AT + SSM_HEADS]
                             .rearrange("(k p) n -> p k n", p=P)).then_inc(dtw_full.sem, 16)
                ffn(l, 0, w1g, w1u, w1d)
                for n in range(N_MIX):
                    slot, use = SLOT_OF[n % 3], use_of(n)
                    if n < N_ATT:
                        load(l, slot, use, w_in, D_MODEL, 0, D_MODEL, COLS[n], PC)
                    elif n < N_SSM:
                        load(l, slot, use, w_att, ATT_DIM, 0, ATT_DIM, (n - N_ATT) * 512, 512)
                    elif n < N_OUT:
                        load(l, slot, use, w_ssm, D_INNER, (n - N_SSM) * PC, PC, 0, D_MODEL)
                    else:
                        load(l, slot, use, w_out, D_MODEL, 0, D_MODEL, (n - N_OUT) * PC, PC)
                ffn(l, USES - FI, w2g, w2u, w2d)

            sp.wait_ge(fin_dve, 2)
            sp.dma_start(out.rearrange("b (t p) n -> p (b t) n", p=P),
                         v_flat[:, 0:KT * SEQ].rearrange("p (t n) -> p t n", t=TILES)).then_inc(stored, 16)
            sp.wait_ge(stored, 16)

        @block.gpsimd
        def _(pool):
            pool.sem_inc(lo_ready[UP_SLOT].sem, 1)
            pool.wait_ge(ld_rest, 16)

            def split_lo(l, use, times=1):
                s = UP_SLOT
                pool.wait_ge(hi_ready[s].sem, hi_ready[s].at(l, use + 1))
                nc.gpsimd.tensor_tensor(wL[s][:, :], raw[s][:, :], wH[s][:, :], ALU.subtract).then_inc(*lo_ready[s].one(times))

            def split_lo_qk(l, use):
                s = UP_SLOT
                pool.wait_ge(hi_ready[s].sem, hi_ready[s].at(l, use + 1))
                for f in range(2):
                    ins = nc.gpsimd.tensor_tensor(halves_out(wL[s], f), halves_in(raw[s], f), halves_out(wH[s], f), ALU.subtract)
                ins.then_inc(*lo_ready[s].one())

            def rope_products(l, i):
                cs = con[:, K_CS:K_CS + 512].rearrange("p (a t) -> p a t", a=2)
                pool.wait_ge(qn_ready.sem, qn_ready.at(l, i + 1))
                if i >= 1:
                    pool.wait_ge(rope_ready.sem, rope_ready.at(l, i))
                nc.gpsimd.tensor_tensor(ropa[:, :, :], qn[i % 2][:, 0:1, :].to_broadcast([P, 2, SEQ]), cs, ALU.mult)
                nc.gpsimd.tensor_tensor(ropb[:, :, :], qn[i % 2][:, 1:2, :].to_broadcast([P, 2, SEQ]), cs, ALU.mult).then_inc(*rope_ab.one())

            def add_squares(l, i):
                pool.wait_ge(proj_read.sem, proj_read.at(l, i + 1))
                q = qsq[i % 2]
                nc.gpsimd.tensor_tensor(q[:, 0:SEQ], q[:, 0:SEQ], q[:, SEQ:512], ALU.add).then_inc(*qsq_added.one())

            def add_y_squares(l, g):
                a, b = sq[:, 2 * (g % 2), :], sq[:, 2 * (g % 2) + 1, :]
                pool.wait_ge(ysq_ready.sem, ysq_ready.at(l, g + 1))
                nc.gpsimd.tensor_tensor(a, a, b, ALU.add).then_inc(*ysq_added.one())
                pool.wait_ge(ysq_added.sem, ysq_added.at(l, 2 * g + 1))
                nc.gpsimd.tensor_tensor(a[:, 0:SEQ], a[:, 0:SEQ], a[:, SEQ:512], ALU.add).then_inc(*ysq_added.one())

            def norm_lo(l, k):
                for c in range(1, KT, 2):
                    pool.wait_ge(hhi.sem, hhi.at(l, KT * k + c + 1))
                    nc.gpsimd.tensor_tensor(hL[:, c, :], ht[:, c, :], hH[:, c, :], ALU.subtract).then_inc(*hlo[1].one())

            def ffn(l, f):
                use0 = (0, USES - FI)[f]
                if f == 0:
                    pool.wait_ge(hi_ready[GATE_SLOT].sem, hi_ready[GATE_SLOT].at(l, 1))
                    nc.gpsimd.tensor_tensor(wL[GATE_SLOT][:, :], raw[GATE_SLOT][:, :], wH[GATE_SLOT][:, :],
                                            ALU.subtract).then_inc(*lo_ready[GATE_SLOT].one())
                split_lo(l, use0)
                if f:
                    norm_lo(l, 2)
                with pool.Fori(1, FI) as i:
                    split_lo(l, use0 + i, FI - 1)

            with pool.Fori(0, DEPTH) as l:
                ffn(l, 0)
                for s in range(-2, N_MIX - 2):
                    if s == 0:
                        norm_lo(l, 1)
                    if s - N_G in (1, 3):
                        add_y_squares(l, s - N_G - 1)
                        add_y_squares(l, s - N_G)
                    n = s + 2
                    if SLOT_OF[n % 3] == UP_SLOT:
                        (split_lo_qk if N_QK <= n < N_V else split_lo)(l, use_of(n))
                    if 0 <= s - N_QK < 12:
                        add_squares(l, s - N_QK)
                    if 0 <= s - 2 - N_QK < 12:
                        rope_products(l, s - 2 - N_QK)
                ffn(l, 1)

        @block.scalar
        def _(act):
            act.dma_start(v_flat[:, 0:KT * SEQ].rearrange("p (t n) -> p t n", t=TILES),
                          x.rearrange("b (t p) n -> p (b t) n", p=P)).then_inc(ld_x, 16)
            act.dma_start(rows_b[24:40, :, :], ssm_w.rearrange("l (c p) -> c l p", p=P)).then_inc(ld_prm, 16)
            act.dma_start(rows_b[40:56, :, :], b_gates.rearrange("l (c p) -> c l p", p=P)).then_inc(ld_prm, 16)
            rr = row_r[:, :].rearrange("a (l n) -> a l n", l=DEPTH)
            for src, lo, hi in ((d_skip, 0, 32), (dt_bias, 32, 64), (a_log, 64, 96), (q_norm, 96, 160), (k_norm, 160, 224)):
                act.dma_start(rr[:, :, lo:hi], src.rearrange("(a l) n -> a l n", a=1)).then_inc(ld_prm, 16)
            act.dma_start(con_tail, consts[:, NKEPT:NCONST]).then_inc(ld_sel, 16)
            act.dma_start(con[:, NEARLY:NKEPT], consts[:, NEARLY:NKEPT]).then_inc(ld_rest, 16)

            def split_hi(l, s, use, times=1):
                act.wait_ge(raw_full[s].sem, raw_full[s].at(l, use + 1))
                act.wait_ge(used[s].sem, used[s].at(l, use))
                act.activation(wH[s][:, :], raw[s][:, :], ACT.Copy).then_inc(*hi_ready[s].one(times))

            def split_mix(l, n):
                s, use = SLOT_OF[n % 3], use_of(n)
                if not N_QK <= n < N_V:
                    return split_hi(l, s, use)
                act.wait_ge(raw_full[s].sem, raw_full[s].at(l, use + 1))
                act.wait_ge(used[s].sem, used[s].at(l, use))
                for f in range(2):
                    ins = act.activation(halves_out(wH[s], f), halves_in(raw[s], f), ACT.Copy)
                ins.then_inc(*hi_ready[s].one())

            def squares(l, k):
                for j in range(4):
                    act.wait_ge(x_ready.sem, x_ready.at(l, 4 * k + j + 1))
                    act.activation(sq[:, j, :].rearrange("p (c t) -> p c t", c=2), xT[:, 2 * j:2 * j + 2, :], ACT.Square).then_inc(*sq_ready.one())

            def inverse_rms(l, k):
                act.preload_act_table_set(LN_EXP)
                act.wait_ge(ss_done.sem, ss_done.at(l, k + 1))
                if k == 0:
                    act.wait_ge(prm_ready.sem, prm_ready.at(l, 1))
                act.activation(rstd[:, :], bank(6, 0, SEQ), ACT.Ln, bias=eps[:, :], scale=1.0 / D_MODEL).then_inc(*ln_done.one())
                act.wait_ge(ln_done.sem, ln_done.at(l, k + 1))
                act.activation(rstd[:, :], rstd[:, :], ACT.Exp, scale=-0.5).then_inc(*rstd_ready.one())

            def h_hi(l, k):
                for c in range(KT):
                    act.wait_ge(hn_ready.sem, hn_ready.at(l, KT * k + c + 1))
                    if k == 2 and c < KT - 1:
                        act.wait_ge(mix_passed.sem, mix_passed.at(l, c + 1))
                    elif k == 2:
                        s = SLOT_OF[(N_MIX - 1) % 3]
                        act.wait_ge(used[s].sem, used[s].at(l, use_of(N_MIX - 1) + 1))
                    act.activation(hH[:, c, :], ht[:, c, :], ACT.Copy).then_inc(*hhi.one())

            def ffn(l, f):
                use0, e0, h0 = (0, USES - FI)[f], f * FI, f * (FI + 1)

                def hid_hi(i, times=1, cols=slice(0, 512)):
                    act.wait_ge(hid_ready.sem, hid_ready.at(l, h0 + i + 1))
                    act.activation(hidH[:, cols], hid[:, cols], ACT.Copy).then_inc(*hidhi.one(times))

                def silu(i, times=1):
                    act.wait_ge(gate_scaled.sem, gate_scaled.at(l, e0 + i + 1))
                    act.activation(sg[:, :], sg[:, :], ACT.Silu).then_inc(*silu_done.one(times))

                split_hi(l, GATE_SLOT, use0)
                split_hi(l, UP_SLOT, use0)
                h_hi(l, 2 * f)
                squares(l, 2 * f)
                split_hi(l, GATE_SLOT, use0 + 1)
                inverse_rms(l, 2 * f)
                silu(0)
                split_hi(l, DOWN_SLOT, use0)
                with act.Fori(1, FI - 1) as i:
                    hid_hi(i - 1, FI - 2)
                    split_hi(l, UP_SLOT, use0 + i, FI - 2)
                    silu(i, FI - 2)
                    split_hi(l, GATE_SLOT, use0 + i + 1, FI - 2)
                    split_hi(l, DOWN_SLOT, use0 + i, FI - 2)
                hid_hi(FI - 2)
                split_hi(l, UP_SLOT, use0 + FI - 1)
                silu(FI - 1)
                split_hi(l, DOWN_SLOT, use0 + FI - 1)
                if f == 0:
                    split_mix(l, 0)
                for c in range(2):
                    hid_hi(FI - 1 + c, cols=slice(c * SEQ, (c + 1) * SEQ))

            def panel_done(l, n):
                s = SLOT_OF[n % 3]
                act.wait_ge(used[s].sem, used[s].at(l, use_of(n) + 1))

            def dt_steps(l):
                act.wait_ge(dt_dve.sem, dt_dve.at(l, 1))
                act.activation(dtu[:, :], dts[:, :], ACT.Abs).then_inc(*dt_act.one())
                act.wait_ge(dt_act.sem, dt_act.at(l, 1))
                act.activation(dte[:, :], dtu[:, :], ACT.Exp, scale=-1.0).then_inc(*dt_act.one())
                act.wait_ge(dt_act.sem, dt_act.at(l, 2))
                act.activation(dtl[:, :], dte[:, :], ACT.Ln, bias=ones[:, 0:1]).then_inc(*dt_act.one())
                act.activation(aexp[:, :], prm[:, C_ALOG:C_ALOG + 32], ACT.Exp).then_inc(*dt_act.one())

            def evacuate(l, n):
                b = 4 + n % 2
                panel_done(l, n)
                if n < N_QK:
                    ch = 2 * XBC_P[n]
                    if n >= 2:
                        act.wait_ge(conv_silu.sem, conv_silu.at(l, n - 1))
                    for j in range(2):
                        act.activation(acc[n % 2][:, j * SEQ:(j + 1) * SEQ], bank(b, j * SEQ, (j + 1) * SEQ), ACT.Identity,
                                       bias=prm[:, C_CONVB + ch + j:C_CONVB + ch + j + 1],
                                       scale=prm[:, C_CONVW + 72 + ch + j:C_CONVW + 73 + ch + j]).then_inc(*conv_bias.one())
                elif n < N_V:
                    i = n - N_QK
                    if i >= 2:
                        act.wait_ge(qn_ready.sem, qn_ready.at(l, i - 1))
                        act.wait_ge(qk_ss.sem, qk_ss.at(l, i - 1))
                    else:
                        act.wait_ge(conv_silu.sem, conv_silu.at(l, N_QK - 1 + i))
                    act.activation(qraw[i % 2][:, :], bank(b), ACT.Copy)
                    act.activation(qsq[i % 2], bank(b), ACT.Square).then_inc(*proj_read.one())
                elif n < N_Z:
                    c0 = (n - N_V) * PC
                    act.activation(v[:, :, c0:c0 + PC], bank(b).rearrange("p (t c) -> p t c", t=TILES), ACT.Copy).then_inc(*proj_read.one())
                elif n < N_G:
                    i = n - N_Z
                    if i >= 2:
                        act.wait_ge(yz_ready.sem, yz_ready.at(l, i - 1))
                    else:
                        act.wait_ge(qk_ss.sem, qk_ss.at(l, 12))
                    act.activation(zs[i % 2][:, :], bank(b), ACT.Silu).then_inc(*proj_read.one())
                elif n < N_ATT:
                    i = n - N_G
                    act.wait_ge(s_done.sem, s_done.at(l, SLOTS))
                    for j in range(2):
                        ins = act.activation(gates[:, 2 * i + j, :], bank(b, j * SEQ, (j + 1) * SEQ), ACT.Sigmoid,
                                             bias=prm[:, C_BG + 2 * i + j:C_BG + 2 * i + j + 1])
                    ins.then_inc(*proj_read.one())

            def conv_out(l, n):
                c0 = 2 * XBC_P[n]
                dst = xs[:, c0:c0 + 2, :] if c0 < 16 else bc[:, c0 - 16:c0 - 14, :]
                act.wait_ge(conv_tap.sem, conv_tap.at(l, 6 * n + 6))
                act.activation(dst, acc[n % 2][:, :].rearrange("p (c t) -> p c t", c=2), ACT.Silu).then_inc(*conv_silu.one())

            def qk_rms(l, i):
                act.wait_ge(qk_ss.sem, qk_ss.at(l, i + 1))
                if i >= 2:
                    act.wait_ge(qn_ready.sem, qn_ready.at(l, i - 1))
                act.activation(qrs[i % 2][:, :], bank(6, (i % 2) * SEQ, (i % 2 + 1) * SEQ), ACT.Ln, bias=eps[:, :],
                               scale=1.0 / HEAD_DIM).then_inc(*qk_ln.one())
                act.wait_ge(qk_ln.sem, qk_ln.at(l, i + 1))
                act.activation(qrs[i % 2][:, :], qrs[i % 2][:, :], ACT.Exp, scale=-0.5).then_inc(*qk_rstd.one())

            def decays(l, k):
                act.wait_ge(decay_sum.sem, decay_sum.at(l, k + 1))
                if k >= 1:
                    act.wait_ge(y_done.sem, y_done.at(l, k))
                for hh in range(2):
                    head, o = 2 * k + hh, hh * SEQ
                    act.activation(dec[:, hh, 0:256], bank(k % 2, o, o + SEQ), ACT.Relu, bias=cumk[:, head:head + 1], scale=-1.0)
                    ins = act.activation(dec[:, hh, 256:384], bank(k % 2, o + P, o + SEQ), ACT.Relu,
                                         bias=cumk[:, 32 + head:33 + head], scale=-1.0)
                ins.then_inc(*dec_diff.one())
                act.wait_ge(dec_diff.sem, dec_diff.at(l, k + 1))
                act.activation(dec[:, :, :], dec[:, :, :], ACT.Exp, scale=-1.0).then_inc(*dec_ready.one())

            def copy_pt(l, sl):
                act.wait_ge(pt_done.sem, pt_done.at(l, sl + 1))
                if sl >= 1:
                    act.wait_ge(pv_done.sem, pv_done.at(l, sl))
                act.activation(pt[:, 0:512], bank(3), ACT.Copy).then_inc(*pt_act.one())

            def attn_hi(l):
                act.wait_ge(att_turned.sem, att_turned.at(l, 1))
                act.activation(attH[:, :, :], att_turned_out, ACT.Copy).then_inc(*att_hi.one())

            def softmax_exp(l, sl):
                act.wait_ge(negm_ready.sem, negm_ready.at(l, sl + 1))
                if sl >= 1:
                    act.wait_ge(p_inv.sem, p_inv.at(l, sl))
                act.activation(sm[:, 0:384], sm[:, 0:384], ACT.Exp, bias=negm[:, 0:1], scale=SCALE, accum_out=psum_[:, 0:1])
                act.activation(sm[:, 384:1152], sm[:, 384:1152], ACT.Exp, bias=negm[:, 1:2], scale=SCALE,
                               accum_out=psum_[:, 1:2]).then_inc(*p_exp.one())

            def y_square(l, g):
                act.wait_ge(yz_ready.sem, yz_ready.at(l, 8))
                if g >= 2:
                    act.wait_ge(yss_done.sem, yss_done.at(l, g - 1))
                act.activation(sq[:, 2 * (g % 2):2 * (g % 2) + 2, :].rearrange("p a (c t) -> p (a c) t", c=2),
                               xs[:, 4 * g:4 * g + 4, :], ACT.Square).then_inc(*ysq_ready.one())

            def y_rms(l, pair):
                act.preload_act_table_set(LN_EXP)
                act.wait_ge(yss_done.sem, yss_done.at(l, 2 * pair + 2))
                if pair:
                    act.wait_ge(yn_ready.sem, yn_ready.at(l, 2))
                act.activation(qrs2[:, :, :], y_sums, ACT.Ln, bias=eps[:, :], scale=1.0 / 512).then_inc(*ysln.one())
                act.wait_ge(ysln.sem, ysln.at(l, pair + 1))
                act.activation(qrs2[:, :, :], qrs2[:, :, :], ACT.Exp, scale=-0.5).then_inc(*yrstd.one())

            def y_hi(l, g):
                act.wait_ge(yn_ready.sem, yn_ready.at(l, g + 1))
                if g >= 2:
                    n = N_SSM + 2 * (g - 2) + 1
                    panel_done(l, n)
                act.activation(yH[:, g % 2, :, :], xs[:, 4 * g:4 * g + 4, :], ACT.Copy).then_inc(*yhi.one())

            def mixer(l):
                split_mix(l, 1)
                act.wait_ge(dtw_full.sem, dtw_full.at(l, 1))
                act.activation(dtwH[:, :], dtw[:, :], ACT.Copy).then_inc(*dtw_hi.one())
                squares(l, 1)
                inverse_rms(l, 1)
                h_hi(l, 1)
                for s in range(N_OUT):
                    if s == 2:
                        dt_steps(l)
                    if 0 <= s - 1 < N_ATT:
                        evacuate(l, s - 1)
                    if 0 <= s - 2 < N_QK:
                        conv_out(l, s - 2)
                    if s == 5:
                        act.wait_ge(cum_done.sem, cum_done.at(l, 1))
                        act.activation(cumr[0:32, :], bank(7, 64, 320, 0, 32), ACT.Copy).then_inc(*dt_act.one())
                    t = s - N_QK
                    if t == 2:
                        act.preload_act_table_set(LN_EXP)
                    if 0 <= t - 2 < 12:
                        qk_rms(l, t - 2)
                    if 0 <= t - 1 < 16:
                        decays(l, t - 1)
                    u = s - N_Z
                    if 0 <= u - 1 < SLOTS:
                        copy_pt(l, u - 1)
                    if u == SLOTS + 3:
                        attn_hi(l)
                    if 0 <= u < SLOTS:
                        softmax_exp(l, u)
                    w = s - N_G
                    if w in (1, 3):
                        y_square(l, w - 1)
                        y_square(l, w)
                    if w in Y_SUMS:
                        y_rms(l, Y_SUMS.index(w))
                    if s in Y_SPLIT:
                        y_hi(l, Y_SPLIT.index(s))
                    if s + 2 <= N_OUT:
                        split_mix(l, s + 2)
                for j in range(3):
                    mixed_hi(l, j)
                split_mix(l, N_OUT + 1)
                mixed_hi(l, 3)
                for n in range(N_OUT + 2, N_MIX):
                    split_mix(l, n)

            def mixed_hi(l, j):
                act.wait_ge(mix_ready.sem, mix_ready.at(l, j + 1))
                act.activation(hH[:, 2 * j:2 * j + 2, :], gates[:, 2 * j:2 * j + 2, :], ACT.Copy).then_inc(*mix_hi.one())

            with act.Fori(0, DEPTH) as l:
                ffn(l, 0)
                mixer(l)
                ffn(l, 1)

        @block.vector
        def _(dve):
            dve.sem_inc(lo_ready[0].sem, 1)
            dve.sem_inc(lo_ready[1].sem, 1)
            dve.sem_inc(dtw_lo.sem, 1)
            dve.memset(eps[:, :], EPS)
            for j in range(4):
                dve.wait_ge(pro_pe, 1 + j)
                dve.tensor_copy(xT[:, 2 * j:2 * j + 2, :], bank(j).rearrange("p (c t) -> p c t", c=2)).then_inc(x_ready.sem, 1)
            dve.wait_ge(pro_pe, 5)
            for l in range(DEPTH):
                c = l * NPRM
                dve.tensor_copy(prm_all[:, c:c + 120], bank(4, l * 120, l * 120 + 120))
                dve.tensor_copy(prm_all[:, c + 120:c + 176], bank(4, 240 + l * 56, 296 + l * 56))
                for r in range(2):
                    dve.tensor_copy(prm_all[64 * r:64 * r + 64, c + C_DSK:c + C_DSK + 16],
                                    bank(5, l * 96, l * 96 + 32, 64 * r, 64 * r + 64).rearrange("p (c r) -> p c r", r=2)[:, :, r])
                dve.tensor_copy(prm_all[:, c + C_DTB:c + C_DTB + 64], bank(5, l * 96 + 32, l * 96 + 96))
                ins = dve.tensor_copy(prm_all[:, c + C_QK:c + C_QK + 4], bank(5, 192 + 4 * l, 196 + 4 * l))
            ins.then_inc(pro_dve, 1)
            dve.wait_ge(pro_dve, 1)
            dve.wait_ge(ld_rest, 16)
            dve.wait_ge(ld_sel, 16)
            dve.tensor_copy(con_r[:, :], con_tail).then_inc(con_ready, 1)

            def split_lo(l, s, use, times=1):
                dve.wait_ge(hi_ready[s].sem, hi_ready[s].at(l, use + 1))
                dve.tensor_tensor(wL[s][:, :], raw[s][:, :], wH[s][:, :], ALU.subtract).then_inc(*lo_ready[s].one(times))

            def split_mix(l, n):
                s = SLOT_OF[n % 3]
                if s == UP_SLOT:
                    return
                if not N_QK <= n < N_V:
                    return split_lo(l, s, use_of(n))
                dve.wait_ge(hi_ready[s].sem, hi_ready[s].at(l, use_of(n) + 1))
                for f in range(2):
                    ins = dve.tensor_tensor(halves_out(wL[s], f), halves_in(raw[s], f), halves_out(wH[s], f), ALU.subtract)
                ins.then_inc(*lo_ready[s].one())

            def residual(l, r, scale, only=None):
                for j in range(4) if only is None else (only,):
                    if r == 1:
                        n = N_OUT + j
                        dve.wait_ge(used[SLOT_OF[n % 3]].sem, used[SLOT_OF[n % 3]].at(l, use_of(n) + 1))
                    elif j < 3:
                        dve.wait_ge(acc_done.sem, acc_done.at(l, 3 * (r // 2) + j + 1))
                    else:
                        dve.wait_ge(used[DOWN_SLOT].sem, used[DOWN_SLOT].at(l, USES if r else FI))
                    xj = xT[:, 2 * j:2 * j + 2, :]
                    dve.scalar_tensor_tensor(out=xj, in0=bank(j).rearrange("p (c t) -> p c t", c=2), scalar=scale, in1=xj,
                                             op0=ALU.mult, op1=ALU.add).then_inc(*x_ready.one())

            def h_lo(l, k, c):
                dve.wait_ge(hhi.sem, hhi.at(l, KT * k + c + 1))
                dve.tensor_tensor(hL[:, c, :], ht[:, c, :], hH[:, c, :], ALU.subtract).then_inc(*hlo[c % 2].one())

            def add_late_squares(l, k):
                for j in (2, 3):
                    dve.wait_ge(sq_ready.sem, sq_ready.at(l, 4 * k + j + 1))
                    dve.tensor_tensor(sq[:, j, 0:SEQ], sq[:, j, 0:SEQ], sq[:, j, SEQ:512], ALU.add).then_inc(*sq_added.one())

            def norm(l, k, col):
                add_late_squares(l, k)
                dve.wait_ge(rstd_ready.sem, rstd_ready.at(l, k + 1))
                for c in range(KT):
                    dve.scalar_tensor_tensor(out=ht[:, c, :], in0=xT[:, c, :], scalar=prm[:, col + c:col + c + 1],
                                             in1=rstd[:, :], op0=ALU.mult, op1=ALU.mult).then_inc(*hn_ready.one())
                    if c % 2:
                        h_lo(l, k, c - 1)

            def scaled_x(l, f):
                k, col = 2 * f, C_N2 if f else C_N1
                for j in range(4):
                    if f:
                        residual(l, 1, 1.0, j)
                    dve.wait_ge(x_ready.sem, x_ready.at(l, 4 * k + j + 1))
                    for c in (2 * j, 2 * j + 1):
                        dve.tensor_scalar(ht[:, c, :], xT[:, c, :], prm[:, col + c:col + c + 1], None, ALU.mult).then_inc(*hn_ready.one())
                        if c >= 1 and (f == 0 or c % 2):
                            h_lo(l, k, c - 1)
                if f == 0:
                    h_lo(l, k, KT - 1)

            def ffn(l, f):
                use0, e0, h0 = (0, USES - FI)[f], f * FI, f * (FI + 1)

                rstd2 = rstd[:, :].rearrange("p (a t) -> p a t", a=1).to_broadcast([P, 2, SEQ])
                two = lambda t: t.rearrange("p (a t) -> p a t", a=2)

                def scale_gate(i, times=1):
                    dve.wait_ge(used[GATE_SLOT].sem, used[GATE_SLOT].at(l, use0 + i + 1))
                    dve.tensor_tensor(two(sg), two(bank(4)), rstd2, ALU.mult).then_inc(*gate_scaled.one(times))

                def scale_silu(i, times=1):
                    dve.wait_ge(silu_done.sem, silu_done.at(l, e0 + i + 1))
                    dve.tensor_tensor(two(sg), two(sg), rstd2, ALU.mult).then_inc(*silu_scaled.one(times))
                    dve.wait_ge(silu_scaled.sem, silu_scaled.at(l, e0 + i + 1))

                def hidden(i, times=1):
                    dve.wait_ge(used[UP_SLOT].sem, used[UP_SLOT].at(l, use0 + i + 1))
                    dve.tensor_tensor(hid[:, :], bank(5), sg[:, :], ALU.mult).then_inc(*hid_ready.one(times))
                    dve.wait_ge(hidhi.sem, hidhi.at(l, h0 + i + 1))
                    dve.tensor_tensor(hidL[:, :], hid[:, :], hidH[:, :], ALU.subtract).then_inc(*hidlo.one(times))

                def last_hidden():
                    for c in range(2):
                        cols = slice(c * SEQ, (c + 1) * SEQ)
                        if c == 0:
                            dve.wait_ge(up_part.sem, up_part.at(l, f + 1))
                        else:
                            dve.wait_ge(used[UP_SLOT].sem, used[UP_SLOT].at(l, use0 + FI))
                        dve.tensor_tensor(hid[:, cols], bank((5, 7)[c], 0, SEQ), sg[:, cols], ALU.mult).then_inc(*hid_ready.one())
                        dve.wait_ge(hidhi.sem, hidhi.at(l, h0 + FI + c))
                        dve.tensor_tensor(hidL[:, cols], hid[:, cols], hidH[:, cols], ALU.subtract).then_inc(*hidlo.one())

                if f:
                    split_lo(l, GATE_SLOT, use0)
                scaled_x(l, f)
                add_late_squares(l, 2 * f)
                split_lo(l, GATE_SLOT, use0 + 1)
                dve.wait_ge(rstd_ready.sem, rstd_ready.at(l, 2 * f + 1))
                scale_gate(0)
                split_lo(l, DOWN_SLOT, use0)
                with dve.Fori(1, FI - 1) as i:
                    scale_silu(i - 1, FI - 2)
                    hidden(i - 1, FI - 2)
                    scale_gate(i, FI - 2)
                    split_lo(l, GATE_SLOT, use0 + i + 1, FI - 2)
                    split_lo(l, DOWN_SLOT, use0 + i, FI - 2)
                scale_silu(FI - 2)
                hidden(FI - 2)
                scale_gate(FI - 1)
                scale_silu(FI - 1)
                split_lo(l, DOWN_SLOT, use0 + FI - 1)
                last_hidden()

            def taps(l, n):
                b, ch = 4 + n % 2, 2 * XBC_P[n]
                for d in range(1, TAPS):
                    for j in range(2):
                        k = 2 * (d - 1) + j
                        if d == 1:
                            dve.wait_ge(conv_bias.sem, conv_bias.at(l, 2 * n + 2))
                        else:
                            dve.wait_ge(conv_tap.sem, conv_tap.at(l, 6 * n + k - 1))
                        a = acc[n % 2][:, j * SEQ + d:(j + 1) * SEQ]
                        col = C_CONVW + (TAPS - 1 - d) * 24 + ch + j
                        dve.scalar_tensor_tensor(out=a, in0=bank(b, j * SEQ, (j + 1) * SEQ - d), scalar=prm[:, col:col + 1], in1=a,
                                                 op0=ALU.mult, op1=ALU.add).then_inc(*conv_tap.one())

            def qk_norm(l, i):
                w = C_QK + 2 * (i // 6)
                dve.wait_ge(qk_rstd.sem, qk_rstd.at(l, i + 1))
                if i >= 2:
                    dve.wait_ge(rope_ab.sem, rope_ab.at(l, i - 1))
                for f in range(2):
                    ins = dve.scalar_tensor_tensor(out=qn[i % 2][:, f, :], in0=qraw[i % 2][:, f * SEQ:(f + 1) * SEQ],
                                                   scalar=prm[:, w + f:w + f + 1], in1=qrs[i % 2][:, :], op0=ALU.mult, op1=ALU.mult)
                ins.then_inc(*qn_ready.one())

            def rope(l, i):
                which, c = i // 6, i % 6
                dve.wait_ge(rope_ab.sem, rope_ab.at(l, i + 1))
                for h in range(4):
                    r, to = slice(32 * h, 32 * h + 32), 64 * (h % 2)
                    chunk = 2 * c + h // 2
                    dve.tensor_tensor(qk[to:to + 32, which, chunk, :], ropa[r, 0, :], ropb[r, 1, :], ALU.subtract)
                    ins = dve.tensor_tensor(qk[to + 32:to + 64, which, chunk, :], ropb[r, 0, :], ropa[r, 1, :], ALU.add)
                ins.then_inc(*rope_ready.one())

            def x_times_dt(l, g, tile):
                dve.wait_ge(xt_done.sem, xt_done.at(l, 2 * g + tile + 1))
                d = dt[:, 32 * tile + 8 * g:32 * tile + 8 * g + 8].rearrange("p (h a) -> p h a", a=1).to_broadcast([P, 8, 64])
                dve.tensor_tensor(xdt[:, g, tile, :].rearrange("p (h c) -> p h c", h=8),
                                  bank(3).rearrange("p (h c) -> p h c", h=8), d, ALU.mult).then_inc(*xdt_ready.one())

            def mask_cb(l, g):
                dve.wait_ge(cb_done.sem, cb_done.at(l, g + 1))
                if g >= 1:
                    dve.wait_ge(l_ready.sem, l_ready.at(l, 4 * g))
                dve.tensor_tensor(cbt[:, 0:256], bank(7, 0, 256), tri, ALU.mult)
                dve.tensor_tensor(cbt[:, 256:384], bank(7, 256, 384), tri[:, 0:P], ALU.mult).then_inc(*cb_copied.one())

            def l_matrices(l, k):
                dve.wait_ge(dec_ready.sem, dec_ready.at(l, k + 1))
                dve.wait_ge(cb_copied.sem, cb_copied.at(l, k // 4 + 1))
                c3 = cbt[:, :].rearrange("p (a n) -> p a n", a=1).to_broadcast([P, 2, 384])
                dve.tensor_tensor(dec[:, :, :], dec[:, :, :], c3, ALU.mult).then_inc(*l_ready.one())

            def y_skip(l, k):
                dve.wait_ge(y_done.sem, y_done.at(l, k + 1))
                dve.scalar_tensor_tensor(out=xs[:, k, :], in0=xs[:, k, :], scalar=prm[:, C_DSK + k:C_DSK + k + 1],
                                         in1=bank(2, (k % 2) * SEQ, (k % 2 + 1) * SEQ), op0=ALU.mult, op1=ALU.add).then_inc(*ys_ready.one())

            def y_gate(l, i):
                dve.wait_ge(proj_read.sem, proj_read.at(l, N_Z - N_QK + i + 1))
                dve.wait_ge(ys_ready.sem, ys_ready.at(l, 16))
                dve.tensor_tensor(xs[:, 2 * i:2 * i + 2, :], xs[:, 2 * i:2 * i + 2, :],
                                  zs[i % 2][:, :].rearrange("p (c t) -> p c t", c=2), ALU.mult).then_inc(*yz_ready.one())

            def copy_pt(l, sl):
                dve.wait_ge(pt_done.sem, pt_done.at(l, sl + 1))
                if sl >= 1:
                    dve.wait_ge(pv_done.sem, pv_done.at(l, sl))
                dve.tensor_copy(pt[:, 1024:1152], bank(2, 256, 384)).then_inc(*pt_last.one())
                dve.tensor_copy(pt[:, 512:1024], bank(6)).then_inc(*pt_dve.one())

            def attn_out(l, sl):
                dve.wait_ge(pv_done.sem, pv_done.at(l, sl + 1))
                for tile in range(TILES):
                    ins = dve.tensor_scalar(att_tok[:, tile, sl * HEAD_DIM:(sl + 1) * HEAD_DIM],
                                            bank(7, tile * HEAD_DIM, (tile + 1) * HEAD_DIM), pinv[sl % 2][:, tile:tile + 1], None, ALU.mult)
                ins.then_inc(*att_tok_ready.one())

            def attn_lo(l):
                dve.wait_ge(att_hi.sem, att_hi.at(l, 1))
                dve.tensor_tensor(attL[:, :, :], att_turned_out, attH[:, :, :], ALU.subtract).then_inc(*att_lo.one())

            def softmax_max(l, sl):
                per_group = lambda t: t.rearrange("p (g k) -> p g k", g=GROUPS)
                mask = per_group(con[:, K_MASK:K_MASK + GROUPS * SEQ])
                dve.wait_ge(pro_dve, 1)
                dve.wait_ge(s_done.sem, s_done.at(l, sl + 1))
                dve.tensor_tensor_reduce(per_group(sm[:, 0:384]), per_group(bank(0, 0, 384)), mask[:, :, P:SEQ], 1.0, NEG, ALU.add, ALU.max,
                                         smax[:, 0:1]).then_inc(*smax_ready.one())
                dve.tensor_tensor_reduce(per_group(sm[:, 384:1152]), per_group(psm[:, 512:1280]), mask[:, :, :], 1.0, NEG, ALU.add, ALU.max,
                                         smax[:, 1:2]).then_inc(*smax_ready.one())
                dve.wait_ge(smax_ready.sem, smax_ready.at(l, 2 * sl + 2))
                dve.tensor_scalar(negm[:, :], smax[:, :], -SCALE, None, ALU.mult).then_inc(*negm_ready.one())

            def softmax_inv(l, sl):
                dve.wait_ge(p_exp.sem, p_exp.at(l, sl + 1))
                if sl >= 2:
                    dve.wait_ge(att_tok_ready.sem, att_tok_ready.at(l, sl - 1))
                dve.reciprocal(pinv[sl % 2][:, :], psum_[:, :]).then_inc(*p_inv.one())

            def y_norm(l, g):
                dve.wait_ge(yrstd.sem, yrstd.at(l, g // 2 + 1))
                for c in range(4 * g, 4 * g + 4):
                    ins = dve.scalar_tensor_tensor(out=xs[:, c, :], in0=xs[:, c, :], scalar=prm[:, C_SSM + c:C_SSM + c + 1],
                                                   in1=yrs[g % 2][:, :], op0=ALU.mult, op1=ALU.mult)
                ins.then_inc(*yn_ready.one())

            def y_lo(l, g):
                dve.wait_ge(yhi.sem, yhi.at(l, g + 1))
                dve.tensor_tensor(yL[:, g % 2, :, :], xs[:, 4 * g:4 * g + 4, :], yH[:, g % 2, :, :],
                                  ALU.subtract).then_inc(*ylo.one())

            def gate_att(l, a):
                s = SLOT_OF[(N_ATT + a) % 3]
                dve.wait_ge(used[s].sem, used[s].at(l, use_of(N_ATT + a) + 1))
                dve.wait_ge(proj_read.sem, proj_read.at(l, N_ATT - N_QK))
                for b in (2 * a, 2 * a + 1):
                    dve.tensor_tensor(gates[:, 2 * b:2 * b + 2, :], bank(6 - 2 * a + b % 2).rearrange("p (c t) -> p c t", c=2),
                                      gates[:, 2 * b:2 * b + 2, :], ALU.mult).then_inc(*att_read.one())

            def merge(l, j, between=None):
                if j < 3:
                    dve.wait_ge(ssm_done.sem, ssm_done.at(l, j + 1))
                else:
                    n = N_OUT - 1
                    dve.wait_ge(used[SLOT_OF[n % 3]].sem, used[SLOT_OF[n % 3]].at(l, use_of(n) + 1))
                gs, ga = gates[:, 8 + 2 * j:10 + 2 * j, :], gates[:, 2 * j:2 * j + 2, :]
                dve.tensor_tensor(gs, bank(j).rearrange("p (c t) -> p c t", c=2), gs, ALU.mult).then_inc(*ssm_read.one())
                dve.wait_ge(ssm_read.sem, ssm_read.at(l, j + 1))
                dve.wait_ge(att_read.sem, att_read.at(l, j + 1))
                dve.tensor_tensor(ga, ga, gs, ALU.add).then_inc(*mix_ready.one())
                if between is not None:
                    between()
                dve.wait_ge(mix_hi.sem, mix_hi.at(l, j + 1))
                dve.tensor_tensor(hL[:, 2 * j:2 * j + 2, :], ga, hH[:, 2 * j:2 * j + 2, :], ALU.subtract).then_inc(*mix_lo.one())

            def mixer(l):
                split_mix(l, 0)
                dve.wait_ge(dtw_hi.sem, dtw_hi.at(l, 1))
                dve.tensor_tensor(dtwL[:, :], dtw[:, :], dtwH[:, :], ALU.subtract).then_inc(*dtw_lo.one())
                residual(l, 0, 0.5)
                norm(l, 1, C_NM)
                d3 = lambda t: t[:, :].rearrange("p (t h) -> p t h", t=TILES)
                per_head = lambda t: t.rearrange("p (a h) -> p a h", a=1).to_broadcast([P, TILES, SSM_HEADS])
                for s in range(N_OUT):
                    if s == 1:
                        dve.wait_ge(dt_done.sem, dt_done.at(l, 1))
                        dve.tensor_copy(dth, bank(7, 0, SEQ, 0, SSM_HEADS)).then_inc(*dt_copied.one())
                    if s == 2:
                        dve.wait_ge(dt_turned.sem, dt_turned.at(l, 1))
                        dve.tensor_tensor(d3(dts), bank(7, 320, 384).rearrange("p (t h) -> p t h", t=TILES),
                                          per_head(prm[:, C_DTB:C_DTB + 32]), ALU.add).then_inc(*dt_dve.one())
                        dve.wait_ge(dt_dve.sem, dt_dve.at(l, 1))
                        dve.tensor_scalar(dtm[:, :], dts[:, :], 0.0, None, ALU.max).then_inc(*dt_dve.one())
                    if 0 <= s - 1 < N_QK:
                        taps(l, s - 1)
                    if s == 2:
                        dve.wait_ge(dt_act.sem, dt_act.at(l, 4))
                        dve.wait_ge(dt_dve.sem, dt_dve.at(l, 2))
                        dve.tensor_tensor(dt[:, :], dtm[:, :], dtl[:, :], ALU.add).then_inc(*dt_dve.one())
                        dve.wait_ge(dt_dve.sem, dt_dve.at(l, 3))
                        dve.scalar_tensor_tensor(out=d3(dta), in0=d3(dt), scalar=-1.0, in1=per_head(aexp[:, :]),
                                                 op0=ALU.mult, op1=ALU.mult).then_inc(*dt_dve.one())
                    if s == 5:
                        dve.wait_ge(cum_done.sem, cum_done.at(l, 1))
                        dve.wait_ge(dt_act.sem, dt_act.at(l, 5))
                        dve.tensor_copy(cumk[:, :], bank(7, 320, 384)).then_inc(*dt_dve.one())
                        dve.tensor_tensor(cumr[32:64, :], bank(7, 64, 320, 0, 32), cumr[0:32, :], ALU.subtract).then_inc(*dt_dve.one())
                    t = s - N_QK
                    if 0 <= t - 2 < 12:
                        qk_norm(l, t - 2)
                    if t >= 0 and t % 4 < 2 and t // 4 < SSM_GROUPS:
                        x_times_dt(l, t // 4, t % 4)
                    if 0 <= t - 1 < 16:
                        l_matrices(l, t - 1)
                    if 0 <= t - 2 < 16:
                        y_skip(l, t - 2)
                    if t >= 0 and t % 4 == 0 and t // 4 < SSM_GROUPS:
                        mask_cb(l, t // 4)
                    if 0 <= t - 3 < 12:
                        rope(l, t - 3)
                    u = s - N_Z
                    if 0 <= u - 1 < 8:
                        y_gate(l, u - 1)
                    if 0 <= u - 1 < SLOTS:
                        copy_pt(l, u - 1)
                    if 0 <= u - 2 < SLOTS:
                        attn_out(l, u - 2)
                    if u == SLOTS + 3:
                        attn_lo(l)
                    if 0 <= u < SLOTS:
                        softmax_max(l, u)
                    w = s - N_G
                    if w in Y_SUMS:
                        for g in range(2):
                            y_norm(l, 2 * Y_SUMS.index(w) + g)
                    if s in Y_SPLIT:
                        y_lo(l, Y_SPLIT.index(s))
                    if s in (N_ATT + 1, N_ATT + 2):
                        gate_att(l, s - N_ATT - 1)
                    if s + 2 <= N_OUT:
                        split_mix(l, s + 2)
                    if 0 <= u < SLOTS:
                        softmax_inv(l, u)
                for j in range(3):
                    merge(l, j)
                merge(l, 3, lambda: split_mix(l, N_OUT + 1))
                for n in range(N_OUT + 2, N_MIX):
                    split_mix(l, n)

            with dve.Fori(0, DEPTH) as l:
                dve.tensor_copy(prm[:, :], prm_all[:, bass.ds(l * NPRM, NPRM)]).then_inc(*prm_ready.one())
                dve.wait_ge(prm_ready.sem, prm_ready.at(l, 1))
                ffn(l, 0)
                mixer(l)
                ffn(l, 1)
                residual(l, 2, 0.5)
            for t in range(TILES):
                dve.wait_ge(fin_pe, t + 1)
                dve.tensor_copy(v_flat[:, t * D_MODEL:(t + 1) * D_MODEL], psm[:, 1024 * t:1024 * t + 1024]).then_inc(fin_dve, 1)

        @block.tensor
        def _(pe):
            for s in range(3):
                pe.sem_inc(used[s].sem, 1)
            pe.wait_ge(ld_con, 16)
            pe.wait_ge(ld_x, 16)
            for j in range(4):
                for c in (2 * j, 2 * j + 1):
                    for t in range(TILES):
                        ins = pe.transpose(bank(j, (c % 2) * SEQ + t * P, (c % 2) * SEQ + t * P + P),
                                           v_flat[:, t * D_MODEL + c * P:t * D_MODEL + (c + 1) * P], ident)
                ins.then_inc(pro_pe, 1)
            pe.wait_ge(ld_prm, 16 * 12)
            for l in range(DEPTH):
                pe.transpose(bank(4, l * 120, l * 120 + 120), rows_a[:, l, :], ident[0:ROWS_A, 0:ROWS_A])
                pe.transpose(bank(4, 240 + l * 56, 296 + l * 56), rows_b[:, l, :], ident[0:ROWS_B, 0:ROWS_B])
                pe.matmul(bank(5, l * 96, l * 96 + 96), ones[0:1, :], row_r[0:1, l * NROW:l * NROW + 96], start=True, stop=True)
                for j in range(4):
                    for h in range(4):
                        c = l * NROW + 96 + 32 * j
                        ins = pe.matmul(bank(5, 192 + 4 * l + j, 193 + 4 * l + j, 32 * h, 32 * h + 32),
                                        row_r[0:1, c:c + 32], ones[0:1, 0:1], start=True, stop=True)
            ins.then_inc(pro_pe, 1)

            def split_ready(l, s, use):
                pe.wait_ge(hi_ready[s].sem, hi_ready[s].at(l, use + 1))
                pe.wait_ge(lo_ready[s].sem, lo_ready[s].at(l, use + 1))

            def product(o, wh, wl, xh, xl, first, last, shared=False):
                pe.matmul(o, wh, xh, start=first, stop=False, skip_group_check=shared)
                pe.matmul(o, wh, xl, start=False, stop=False, skip_group_check=shared)
                return pe.matmul(o, wl, xh, start=False, stop=last, skip_group_check=shared)

            def panel(s, b):
                for c in range(2):
                    for k in range(KT):
                        w0 = k * PC + c * P
                        ins = product(bank(b, c * SEQ, (c + 1) * SEQ), wH[s][:, w0:w0 + P], wL[s][:, w0:w0 + P],
                                      hH[:, k, :], hL[:, k, :], k == 0, k == KT - 1)
                return ins

            def first_panel(s, b, hi_of, lo_of, passed=None, late=None):
                def add(k, w, h, first, last):
                    for c in range(2):
                        w0 = k * PC + c * P
                        ins = pe.matmul(bank(b, c * SEQ, (c + 1) * SEQ), w[s][:, w0:w0 + P], h[:, k, :],
                                        start=(first and c == 0), stop=last, skip_group_check=True)
                    return ins

                for k in range(KT):
                    hi_of(k)
                    add(k, wH, hH, k == 0, False)
                    if late is None:
                        add(k, wL, hH, False, False)
                    elif k >= KT // 2:
                        if k == KT // 2:
                            late()
                        add(k - KT // 2, wL, hH, False, False)
                        add(k, wL, hH, False, False)
                    if k >= 1:
                        lo_of(k - 1)
                        ins = add(k - 1, wH, hL, False, False)
                        if passed is not None:
                            passed(ins)
                lo_of(KT - 1)
                return add(KT - 1, wH, hL, False, True)

            def norm_sum(l, k):
                for j in range(4):
                    if j < 2:
                        pe.wait_ge(sq_ready.sem, sq_ready.at(l, 4 * k + j + 1))
                    else:
                        pe.wait_ge(sq_added.sem, sq_added.at(l, 2 * k + j - 1))
                    for c in range(2 if j < 2 else 1):
                        ins = pe.matmul(bank(6, 0, SEQ), ones, sq[:, j, c * SEQ:(c + 1) * SEQ], start=(j == 0 and c == 0),
                                        stop=(j == 3))
                ins.then_inc(*ss_done.one())

            def hi_of_h(l, k):
                return lambda c: pe.wait_ge(hhi.sem, hhi.at(l, KT * k + c + 1))

            def lo_of_h(l, k):
                return lambda c: pe.wait_ge(hlo[c % 2].sem, hlo[c % 2].at(l, KT // 2 * k + c // 2 + 1))

            def ffn(l, f):
                use0, e0, h0 = (0, USES - FI)[f], f * FI, f * (FI + 1)

                def gate(i, times=1):
                    split_ready(l, GATE_SLOT, use0 + i)
                    panel(GATE_SLOT, 4).then_inc(*used[GATE_SLOT].one(times))

                def up(i, times=1):
                    split_ready(l, UP_SLOT, use0 + i)
                    panel(UP_SLOT, 5).then_inc(*used[UP_SLOT].one(times))

                def down_part(c, k, first=False, last=False):
                    w0 = k * D_MODEL + c * P
                    return product(bank(c // 2, (c % 2) * SEQ, (c % 2 + 1) * SEQ),
                                   wH[DOWN_SLOT][:, w0:w0 + P], wL[DOWN_SLOT][:, w0:w0 + P],
                                   hidH[:, k * SEQ:(k + 1) * SEQ], hidL[:, k * SEQ:(k + 1) * SEQ],
                                   first and c % 2 == 0 and k == 0, last, shared=True)

                def down(i, times=1, first=False):
                    split_ready(l, DOWN_SLOT, use0 + i)
                    pe.wait_ge(hidlo.sem, hidlo.at(l, h0 + i + 1))
                    for c in range(KT):
                        for k in range(2):
                            ins = down_part(c, k, first)
                    ins.then_inc(*used[DOWN_SLOT].one(times))

                def last_up():
                    split_ready(l, UP_SLOT, use0 + FI - 1)
                    for c in range(2):
                        for k in range(KT):
                            w0 = k * PC + c * P
                            ins = product(bank((5, 7)[c], 0, SEQ), wH[UP_SLOT][:, w0:w0 + P], wL[UP_SLOT][:, w0:w0 + P],
                                          hH[:, k, :], hL[:, k, :], k == 0, k == KT - 1)
                        ins.then_inc(*(up_part if c == 0 else used[UP_SLOT]).one())

                def last_down():
                    split_ready(l, DOWN_SLOT, use0 + FI - 1)
                    for k in range(2):
                        pe.wait_ge(hidlo.sem, hidlo.at(l, h0 + FI + k))
                        for c in range(KT):
                            ins = down_part(c, k, last=(k == 1))
                            if k == 1 and c in (1, 3, 5):
                                ins.then_inc(*acc_done.one())
                    ins.then_inc(*used[DOWN_SLOT].one())

                lo_wait = lambda: pe.wait_ge(lo_ready[GATE_SLOT].sem, lo_ready[GATE_SLOT].at(l, use0 + 1))
                pe.wait_ge(hi_ready[GATE_SLOT].sem, hi_ready[GATE_SLOT].at(l, use0 + 1))
                if f:
                    lo_wait()
                first_panel(GATE_SLOT, 4, hi_of_h(l, 2 * f), lo_of_h(l, 2 * f),
                            late=None if f else lo_wait).then_inc(*used[GATE_SLOT].one())
                norm_sum(l, 2 * f)
                up(0)
                pe.wait_ge(gate_scaled.sem, gate_scaled.at(l, e0 + 1))
                gate(1)
                down(0, first=True)
                up(1)
                with pe.Fori(2, FI - 1) as i:
                    pe.wait_ge(gate_scaled.sem, gate_scaled.at(l, e0 + i))
                    gate(i, FI - 3)
                    down(i - 1, FI - 3)
                    up(i, FI - 3)
                pe.wait_ge(gate_scaled.sem, gate_scaled.at(l, e0 + FI - 1))
                gate(FI - 1)
                down(FI - 2)
                last_up()
                last_down()

            def dt_product(l):
                pe.wait_ge(dtw_lo.sem, dtw_lo.at(l, 1))
                for k in range(KT):
                    c = slice(k * SSM_HEADS, (k + 1) * SSM_HEADS)
                    ins = product(bank(7, 0, SEQ, 0, SSM_HEADS), dtwH[:, c], dtwL[:, c], hH[:, k, :], hL[:, k, :], k == 0, k == KT - 1)
                ins.then_inc(*dt_done.one())

            def dt_transpose(l):
                pe.wait_ge(dt_copied.sem, dt_copied.at(l, 1))
                for t in range(TILES):
                    ins = pe.matmul(bank(7, 320 + 32 * t, 352 + 32 * t), dth[:, t * P:(t + 1) * P], ident[0:SSM_HEADS, 0:SSM_HEADS],
                                    start=True, stop=True)
                ins.then_inc(*dt_turned.one())

            def cumulate(l):
                pe.wait_ge(dt_dve.sem, dt_dve.at(l, 4))
                pe.matmul(bank(7, 64, 320, 0, 32), dta[:, 0:32], tri, start=True, stop=False)
                pe.matmul(bank(7, 192, 320, 0, 32), dta[:, 32:64], tri[:, 0:P], start=False, stop=True)
                pe.matmul(bank(7, 320, 352), tri[:, 0:P], dta[:, 0:32], start=True, stop=True)
                pe.matmul(bank(7, 352, 384), ones, dta[:, 0:32], start=True, stop=False)
                pe.matmul(bank(7, 352, 384), tri[:, 0:P], dta[:, 32:64], start=False, stop=True).then_inc(*cum_done.one())

            def qk_sum(l, i):
                pe.wait_ge(qsq_added.sem, qsq_added.at(l, i + 1))
                if i >= 1:
                    pe.wait_ge(qk_ln.sem, qk_ln.at(l, i))
                o = bank(6, (i % 2) * SEQ, (i % 2 + 1) * SEQ)
                blk = con[:, K_BLK:K_BLK + P]
                pe.matmul(o, blk, qsq[i % 2][:, 0:SEQ], start=True, stop=True).then_inc(*qk_ss.one())

            def x_transpose(l, g, tile):
                pe.wait_ge(conv_silu.sem, conv_silu.at(l, 6 + 2 * g))
                if g or tile:
                    pe.wait_ge(xdt_ready.sem, xdt_ready.at(l, 2 * g + tile))
                for c in range(4):
                    ins = pe.transpose(bank(3, c * P, (c + 1) * P), xs[:, 4 * g + c, tile * P:(tile + 1) * P], ident)
                ins.then_inc(*xt_done.one())

            def cb(l, g):
                if g == 0:
                    pe.wait_ge(dt_dve.sem, dt_dve.at(l, 6))
                else:
                    pe.wait_ge(cb_copied.sem, cb_copied.at(l, g))
                pe.matmul(bank(7, 0, 256), bc[:, g, 0:P], bc[:, 4 + g, :], start=True, stop=True)
                pe.matmul(bank(7, 256, 384), bc[:, g, P:SEQ], bc[:, 4 + g, P:SEQ], start=True, stop=True).then_inc(*cb_done.one())

            def decay_sums(l, k):
                if k == 0:
                    pe.wait_ge(dt_dve.sem, dt_dve.at(l, 6))
                    pe.wait_ge(con_ready, 1)
                elif k >= 2:
                    pe.wait_ge(dec_diff.sem, dec_diff.at(l, k - 1))
                for hh in range(2):
                    sel = sel_r[0:64, 2 * k + hh:2 * k + hh + 1].to_broadcast([64, P])
                    ins = pe.matmul(bank(k % 2, hh * SEQ, (hh + 1) * SEQ), sel, cumr[:, :], start=True, stop=True)
                ins.then_inc(*decay_sum.one())

            def ssd(l, k):
                g, c0 = k // 4, (k % 4) * P
                pe.wait_ge(l_ready.sem, l_ready.at(l, k + 1))
                pe.wait_ge(xdt_ready.sem, xdt_ready.at(l, 2 * g + 2))
                if k >= 1:
                    pe.wait_ge(ys_ready.sem, ys_ready.at(l, k))
                b0 = (k % 2) * SEQ
                for hh in range(2):
                    r = 64 * hh
                    pe.matmul(bank(2, b0, b0 + SEQ, r, r + 64), xdt[:, g, 0, c0 + r:c0 + r + 64], dec[:, hh, 0:256], start=True, stop=False)
                    ins = pe.matmul(bank(2, b0 + P, b0 + SEQ, r, r + 64), xdt[:, g, 1, c0 + r:c0 + r + 64], dec[:, hh, 256:384],
                                    start=False, stop=True)
                ins.then_inc(*y_done.one())

            def scores(l, sl):
                if sl == 0:
                    pe.wait_ge(rope_ready.sem, rope_ready.at(l, 12))
                    pe.wait_ge(dec_diff.sem, dec_diff.at(l, 16))
                    pe.wait_ge(ys_ready.sem, ys_ready.at(l, 16))
                else:
                    pe.wait_ge(smax_ready.sem, smax_ready.at(l, 2 * sl))
                heads = [divmod(SLOTS * g + sl, 2) for g in range(GROUPS)]
                for g, (c, h) in enumerate(heads):
                    r = slice(64 * h, 64 * h + 64)
                    pe.matmul(bank(0, g * P, (g + 1) * P), qk[r, 0, c, 0:P], qk[r, 1, c, 0:P], start=True, stop=True)
                for g, (c, h) in enumerate(heads):
                    r = slice(64 * h, 64 * h + 64)
                    if g == 2 and sl >= 1:
                        pe.wait_ge(pt_last.sem, pt_last.at(l, sl))
                    ins = pe.matmul(psm[:, 512 + g * SEQ:512 + (g + 1) * SEQ], qk[r, 0, c, P:SEQ], qk[r, 1, c, :],
                                    start=True, stop=True)
                ins.then_inc(*s_done.one())

            def p_transpose(l, sl):
                pe.wait_ge(p_exp.sem, p_exp.at(l, sl + 1))
                if sl == 0:
                    pe.wait_ge(qk_ln.sem, qk_ln.at(l, 12))
                else:
                    pe.wait_ge(pt_act.sem, pt_act.at(l, sl))
                    pe.wait_ge(pt_dve.sem, pt_dve.at(l, sl))
                for i in range(9):
                    g, j = divmod(i, 3)
                    c = (g * P, 384 + g * SEQ, 384 + g * SEQ + P)[j]
                    o = bank(2, 256, 384) if i == 8 else bank((3, 6)[i // 4], (i % 4) * P, (i % 4 + 1) * P)
                    ins = pe.transpose(o, sm[:, c:c + P], ident)
                ins.then_inc(*pt_done.one())

            def p_times_v(l, sl):
                pe.wait_ge(pt_act.sem, pt_act.at(l, sl + 1))
                pe.wait_ge(pt_dve.sem, pt_dve.at(l, sl + 1))
                pe.wait_ge(proj_read.sem, proj_read.at(l, N_Z - N_QK))
                if sl >= 1:
                    pe.wait_ge(att_tok_ready.sem, att_tok_ready.at(l, sl))
                for tile in range(TILES):
                    o = bank(7, tile * HEAD_DIM, (tile + 1) * HEAD_DIM)
                    blocks = [(g, key) for g in range(GROUPS) for key in range(tile + 1)]
                    for g, key in blocks:
                        c, j = g * ATT_DIM + sl * HEAD_DIM, 3 * g + tile + key
                        ins = pe.matmul(o, pt[:, j * P:(j + 1) * P], v[:, key, c:c + HEAD_DIM],
                                        start=((g, key) == blocks[0]), stop=((g, key) == blocks[-1]))
                ins.then_inc(*pv_done.one())

            def att_transpose(l):
                pe.wait_ge(att_tok_ready.sem, att_tok_ready.at(l, SLOTS))
                for c in range(4):
                    for tile in range(TILES):
                        o = c * SEQ + tile * P
                        ins = pe.transpose(psm[:, 1024 + o:1024 + o + P], att_tok[:, tile, c * P:(c + 1) * P], ident)
                ins.then_inc(*att_turned.one())

            def y_sum(l, g):
                pe.wait_ge(ysq_added.sem, ysq_added.at(l, 2 * g + 2))
                if g < 2:
                    pe.wait_ge(smax_ready.sem, smax_ready.at(l, 16))
                else:
                    pe.wait_ge(ysln.sem, ysln.at(l, 1))
                pe.matmul(bank(g % 2, 0, SEQ), ones, sq[:, 2 * (g % 2), 0:SEQ], start=True, stop=True).then_inc(*yss_done.one())

            def bank_free(l, n):
                m = n - 2
                if 0 <= m < N_QK:
                    pe.wait_ge(conv_tap.sem, conv_tap.at(l, 6 * m + 6))
                elif m >= N_QK:
                    pe.wait_ge(proj_read.sem, proj_read.at(l, m - N_QK + 1))

            def ssm_chunk(m, c):
                s, g = SLOT_OF[(N_SSM + m) % 3], m // 2
                for k in range(2):
                    w0, y = k * D_MODEL + c * P, 2 * (m % 2) + k
                    ins = product(bank(c // 2, (c % 2) * SEQ, (c % 2 + 1) * SEQ), wH[s][:, w0:w0 + P], wL[s][:, w0:w0 + P],
                                  yH[:, g % 2, y, :], yL[:, g % 2, y, :], m == 0 and c % 2 == 0 and k == 0,
                                  m == 7 and k == 1, shared=True)
                return ins

            def mixer(l):
                norm_sum(l, 1)
                for n in range(N_ATT):
                    if n == 1:
                        dt_product(l)
                    if n == 2:
                        dt_transpose(l)
                    if n == 4:
                        cumulate(l)
                    t = n - N_QK
                    if 0 <= t - 2 < 12:
                        qk_sum(l, t - 2)
                    if t >= 0 and t % 4 < 2 and t // 4 < SSM_GROUPS:
                        x_transpose(l, t // 4, t % 4)
                    if t >= 0 and t % 4 == 0 and t // 4 < SSM_GROUPS:
                        cb(l, t // 4)
                    if 0 <= t - 1 < 16:
                        decay_sums(l, t - 1)
                    if 0 <= t - 2 < 16:
                        ssd(l, t - 2)
                    u = n - N_Z
                    if 0 <= u - 2 < SLOTS:
                        p_times_v(l, u - 2)
                    if 0 <= u - 1 < SLOTS:
                        p_transpose(l, u - 1)
                    if 0 <= u < SLOTS:
                        scores(l, u)
                    if u == SLOTS + 2:
                        att_transpose(l)
                    w = n - N_G
                    if w in Y_SUMS:
                        for g in range(2):
                            y_sum(l, 2 * Y_SUMS.index(w) + g)
                    s, b = SLOT_OF[n % 3], 4 + n % 2
                    bank_free(l, n)
                    split_ready(l, s, use_of(n))
                    if N_V <= n < N_Z:
                        for tile in range(TILES):
                            for k in range(KT):
                                ts = slice(tile * P, (tile + 1) * P)
                                ins = product(bank(b, tile * PC, (tile + 1) * PC), hH[:, k, ts], hL[:, k, ts],
                                              wH[s][:, k * PC:(k + 1) * PC], wL[s][:, k * PC:(k + 1) * PC], k == 0, k == KT - 1)
                    elif n == 0:
                        ins = first_panel(s, b, hi_of_h(l, 1), lo_of_h(l, 1))
                    else:
                        ins = panel(s, b)
                    ins.then_inc(*used[s].one())
                for a in range(2):
                    n = N_ATT + a
                    s = SLOT_OF[n % 3]
                    split_ready(l, s, use_of(n))
                    if a == 0:
                        pe.wait_ge(att_lo.sem, att_lo.at(l, 1))
                    else:
                        pe.wait_ge(proj_read.sem, proj_read.at(l, N_ATT - N_QK))
                    for c in range(4):
                        for k in range(4):
                            w0 = k * 512 + c * P
                            ins = product(bank(6 - 2 * a + c // 2, (c % 2) * SEQ, (c % 2 + 1) * SEQ), wH[s][:, w0:w0 + P], wL[s][:, w0:w0 + P],
                                          attH[:, k, :], attL[:, k, :], k == 0, k == 3)
                    ins.then_inc(*used[s].one())
                for m in range(6):
                    n, g = N_SSM + m, m // 2
                    s = SLOT_OF[n % 3]
                    split_ready(l, s, use_of(n))
                    pe.wait_ge(ylo.sem, ylo.at(l, g + 1))
                    if m == 0:
                        pe.wait_ge(ysln.sem, ysln.at(l, 2))
                    for c in range(KT):
                        ins = ssm_chunk(m, c)
                    ins.then_inc(*used[s].one())
                last = [SLOT_OF[(N_SSM + m) % 3] for m in (6, 7)]
                split_ready(l, last[0], use_of(N_SSM + 6))
                pe.wait_ge(ylo.sem, ylo.at(l, 4))
                ssm_chunk(6, 0)
                ssm_chunk(6, 1)
                split_ready(l, last[1], use_of(N_SSM + 7))
                for c in range(KT):
                    if c >= 2:
                        ins = ssm_chunk(6, c)
                    if c == KT - 1:
                        ins.then_inc(*used[last[0]].one())
                    ins = ssm_chunk(7, c)
                    if c in (1, 3, 5):
                        ins.then_inc(*ssm_done.one())
                ins.then_inc(*used[last[1]].one())
                for j in range(4):
                    n = N_OUT + j
                    s = SLOT_OF[n % 3]
                    split_ready(l, s, use_of(n))
                    if j == 0:
                        pe.wait_ge(att_read.sem, att_read.at(l, 4))

                        ins = first_panel(s, j, lambda k: pe.wait_ge(mix_hi.sem, mix_hi.at(l, k // 2 + 1)),
                                          lambda k: pe.wait_ge(mix_lo.sem, mix_lo.at(l, k // 2 + 1)))
                    elif j == 3:
                        ins = first_panel(s, j, lambda k: None, lambda k: None, lambda i: i.then_inc(*mix_passed.one()))
                    else:
                        ins = panel(s, j)
                    ins.then_inc(*used[s].one())

            with pe.Fori(0, DEPTH) as l:
                ffn(l, 0)
                mixer(l)
                ffn(l, 1)
            pe.wait_ge(x_ready.sem, 12 * DEPTH + 4)
            for t in range(TILES):
                for c in range(KT):
                    ins = pe.transpose(psm[:, 1024 * t + c * P:1024 * t + (c + 1) * P], xT[:, c, t * P:(t + 1) * P], ident)
                ins.then_inc(fin_pe, 1)

    for s in signals:
        if s.unit == 1:
            assert s.seen == s.per_layer, (s.sem, s.seen, s.per_layer)


_INS = ['x', 'ffn1_norm_w', 'ffn1_w_gate', 'ffn1_w_up', 'ffn1_w_down', 'mix_norm_w', 'w_in', 'b_gates', 'q_norm_w', 'k_norm_w',
        'conv_w', 'conv_b', 'dt_bias', 'a_log', 'd_skip', 'ssm_norm_w', 'w_att_proj', 'w_ssm_proj', 'w_out', 'ffn2_norm_w',
        'ffn2_w_gate', 'ffn2_w_up', 'ffn2_w_down']


def kernel(**inputs):
    import concourse.bacc as _bacc
    from concourse.bass_utils import run_bass_kernel_spmd as _run

    nc = _bacc.Bacc("TRN2", target_bir_lowering=False, num_devices=1)
    arrays, args = {}, []
    for name in _INS:
        arrays[f"in_{name}"] = np.ascontiguousarray(inputs[name])
    arrays["in_constants"] = constants()
    for name, a in arrays.items():
        args.append(nc.dram_tensor(name, a.shape, mybir.dt.from_np(a.dtype), kind="ExternalInput").ap())
    out = nc.dram_tensor("out_0", (1, SEQ, D_MODEL), F32, kind="ExternalOutput").ap()
    program(nc, *args, out)
    r = _run(nc, [arrays], core_ids=[0])
    return r.results[0]["out_0"]
```
